# Optimizing a Trainium2 kernel written in Bass

```python
import jax, jax.numpy as jnp
from jax import lax
import numpy as np

D_MODEL = 1024
BATCH = 1
SEQ = 512
DEPTH = 2

N_A_LAYERS = DEPTH // 2
N_B_LAYERS = DEPTH - N_A_LAYERS
EXPAND = 2
D_INNER = EXPAND * D_MODEL
RMS_EPS = 1e-6
GLA_HEADS = 4
GLA_DK = D_MODEL // 2
GLA_DK_HEAD = GLA_DK // GLA_HEADS
GLA_DV_HEAD = D_INNER // GLA_HEADS
GLA_GATE_RANK = 16
GLA_GATE_TAU = 16.0
GLA_CHUNK = 64
A_IN = 2 * GLA_DK + 2 * D_INNER + GLA_GATE_RANK
DIL_GROUPS = ((128, 1), (512, 4), (2048, 16))
N_GROUPS = len(DIL_GROUPS)
DIL_HEADS = 16
DIL_HEAD_DIM = D_INNER // DIL_HEADS
DIL_BLOCK = 128
ALIBI_MAX_EXP = 8.0
B_IN = N_GROUPS * D_INNER + D_INNER
KV_OUT = 2 * N_GROUPS * D_INNER

kernel_name = "yoco_gla_dilated_alibi_hybrid"

def rmsnorm(x, g):
    xf = x.astype(jnp.float32)
    y = xf * lax.rsqrt(jnp.mean(xf * xf, axis=-1, keepdims=True) + RMS_EPS)
    return (y * g.astype(jnp.float32)).astype(x.dtype)

def gla_mixer(h, w_in, w_gate_up, b_gate, g_out, w_out):
    B, S, _ = h.shape
    H, dk, dv, C = GLA_HEADS, GLA_DK_HEAD, GLA_DV_HEAD, GLA_CHUNK
    n = S // C
    proj = h @ w_in
    q, k, v, z, lr = jnp.split(proj, [GLA_DK, 2 * GLA_DK, 2 * GLA_DK + D_INNER, 2 * GLA_DK + 2 * D_INNER], axis=-1)
    log_a = jax.nn.log_sigmoid((lr @ w_gate_up + b_gate).astype(jnp.float32)) / GLA_GATE_TAU

    def chunks(t, d):
        return t.astype(jnp.float32).reshape(B, n, C, H, d).transpose(1, 0, 3, 2, 4)

    qc = chunks(q, dk) * (dk ** -0.5)
    kc, vc, gc = chunks(k, dk), chunks(v, dv), chunks(log_a, dk)
    causal = jnp.tril(jnp.ones((C, C), dtype=bool))

    def step(state, inp):
        qi, ki, vi, gi = inp
        b = jnp.cumsum(gi, axis=2)
        o_inter = jnp.einsum('bhtk,bhkv->bhtv', qi * jnp.exp(b), state)
        diff = b[:, :, :, None, :] - b[:, :, None, :, :]
        decay = jnp.exp(jnp.where(causal[None, None, :, :, None], diff, -jnp.inf))
        attn = jnp.einsum('bhtk,bhsk,bhtsk->bhts', qi, ki, decay)
        o_intra = jnp.einsum('bhts,bhsv->bhtv', attn, vi)
        b_last = b[:, :, -1:, :]
        k_dec = ki * jnp.exp(b_last - b)
        new_state = jnp.exp(b_last[:, :, 0, :])[..., None] * state + jnp.einsum('bhsk,bhsv->bhkv', k_dec, vi)
        return new_state, o_inter + o_intra

    state0 = jnp.zeros((B, H, dk, dv), jnp.float32)
    _, o = lax.scan(step, state0, (qc, kc, vc, gc))
    o = o.transpose(1, 0, 3, 2, 4).reshape(B, S, H, dv)
    o = o * lax.rsqrt(jnp.mean(o * o, axis=-1, keepdims=True) + RMS_EPS) * g_out.astype(jnp.float32)
    o = o.reshape(B, S, D_INNER) * jax.nn.silu(z.astype(jnp.float32))
    return o.astype(h.dtype) @ w_out

def dilated_group(q, k, v, slopes, window, dilation):
    B, S, H, Dh = q.shape
    d = dilation
    n_steps = window // d
    L = S // d
    blk = DIL_BLOCK
    nb = -(-L // blk)
    Lp = nb * blk

    def to_sub(t):
        t = t.astype(jnp.float32).reshape(B, L, d, H, Dh).transpose(0, 2, 1, 3, 4).reshape(B * d, L, H, Dh)
        return jnp.pad(t, ((0, 0), (0, Lp - L), (0, 0), (0, 0)))

    qs, ks, vs = to_sub(q), to_sub(k), to_sub(v)
    qb = qs.reshape(B * d, nb, blk, H, Dh)

    def band(t):
        tp = jnp.pad(t, ((0, 0), (blk, 0), (0, 0), (0, 0)))
        prev = tp[:, :Lp].reshape(B * d, nb, blk, H, Dh)
        return jnp.concatenate([prev, t.reshape(B * d, nb, blk, H, Dh)], axis=2)

    kb, vb = band(ks), band(vs)
    s = jnp.einsum('znqhd,znkhd->znhqk', qb, kb) * (Dh ** -0.5)
    qi = jnp.arange(blk)[:, None]
    ki = jnp.arange(2 * blk)[None, :]
    delta = qi + blk - ki
    key_pos = jnp.arange(nb)[:, None, None] * blk - blk + ki[None]
    valid = (delta >= 0)[None] & (delta <= n_steps)[None] & (key_pos >= 0)
    bias = -slopes[:, None, None] * (delta * d).astype(jnp.float32)[None]
    s = jnp.where(valid[None, :, None], s + bias[None, None], -jnp.inf)
    m = jnp.max(s, axis=-1, keepdims=True)
    p = jnp.exp(s - m)
    l = jnp.sum(p, axis=-1, keepdims=True)
    o = jnp.einsum('znhqk,znkhd->znhqd', p, vb) / l
    lse = (m + jnp.log(l))[..., 0]
    o = o.transpose(0, 1, 3, 2, 4).reshape(B * d, Lp, H, Dh)[:, :L]
    o = o.reshape(B, d, L, H, Dh).transpose(0, 2, 1, 3, 4).reshape(B, S, H, Dh)
    lse = lse.transpose(0, 1, 3, 2).reshape(B * d, Lp, H)[:, :L]
    lse = lse.reshape(B, d, L, H).transpose(0, 2, 1, 3).reshape(B, S, H)
    return o, lse

def dilated_mixer(h, w_in, k_shared, v_shared, w_out):
    B, S, _ = h.shape
    proj = h @ w_in
    qs = proj[..., :N_GROUPS * D_INNER].reshape(B, S, N_GROUPS, DIL_HEADS, DIL_HEAD_DIM)
    z = proj[..., N_GROUPS * D_INNER:]
    n_all = N_GROUPS * DIL_HEADS
    slopes = (2.0 ** (-ALIBI_MAX_EXP * (jnp.arange(n_all, dtype=jnp.float32) + 1.0) / n_all)).reshape(N_GROUPS, DIL_HEADS)
    outs, lses = [], []
    for g, (window, dilation) in enumerate(DIL_GROUPS):
        o_g, lse_g = dilated_group(qs[:, :, g], k_shared[:, :, g], v_shared[:, :, g], slopes[g], window, dilation)
        outs.append(o_g)
        lses.append(lse_g)
    wts = jax.nn.softmax(jnp.stack(lses, axis=0), axis=0)
    o = jnp.sum(wts[..., None] * jnp.stack(outs, axis=0), axis=0)
    o = o.reshape(B, S, D_INNER) * jax.nn.silu(z.astype(jnp.float32))
    return o.astype(h.dtype) @ w_out

def setup_inputs(seed: int = 0) -> dict:
    key = jax.random.key(seed)
    ks = jax.random.split(key, 14)
    f32 = jnp.float32
    nrm = lambda k, shape, fan: jax.random.normal(k, shape, f32) * (fan ** -0.5)
    return {
        "x": jax.random.normal(ks[0], (BATCH, SEQ, D_MODEL), f32),
        "a_norm": 1.0 + 0.02 * jax.random.normal(ks[1], (N_A_LAYERS, D_MODEL), f32),
        "a_w_in": nrm(ks[2], (N_A_LAYERS, D_MODEL, A_IN), D_MODEL),
        "a_w_gate_up": nrm(ks[3], (N_A_LAYERS, GLA_GATE_RANK, GLA_DK), GLA_GATE_RANK),
        "a_b_gate": 0.1 * jax.random.normal(ks[4], (N_A_LAYERS, GLA_DK), f32),
        "a_g_out": 1.0 + 0.02 * jax.random.normal(ks[5], (N_A_LAYERS, GLA_DV_HEAD), f32),
        "a_w_out": nrm(ks[6], (N_A_LAYERS, D_INNER, D_MODEL), D_INNER),
        "kv_norm": 1.0 + 0.02 * jax.random.normal(ks[7], (D_MODEL,), f32),
        "w_kv": nrm(ks[8], (D_MODEL, KV_OUT), D_MODEL),
        "b_norm": 1.0 + 0.02 * jax.random.normal(ks[9], (N_B_LAYERS, D_MODEL), f32),
        "b_w_in": nrm(ks[10], (N_B_LAYERS, D_MODEL, B_IN), D_MODEL),
        "b_w_out": nrm(ks[11], (N_B_LAYERS, D_INNER, D_MODEL), D_INNER),
        "final_norm": 1.0 + 0.02 * jax.random.normal(ks[12], (D_MODEL,), f32),
    }

def reference(x, a_norm, a_w_in, a_w_gate_up, a_b_gate, a_g_out, a_w_out, kv_norm, w_kv, b_norm, b_w_in, b_w_out, final_norm):
    B, S, _ = x.shape
    k_shared = None
    v_shared = None
    for i in range(DEPTH):
        if i < N_A_LAYERS:
            h = rmsnorm(x, a_norm[i])
            x = x + gla_mixer(h, a_w_in[i], a_w_gate_up[i], a_b_gate[i], a_g_out[i], a_w_out[i])
            if i == N_A_LAYERS - 1:
                kv = (rmsnorm(x, kv_norm) @ w_kv).reshape(B, S, 2, N_GROUPS, DIL_HEADS, DIL_HEAD_DIM)
                k_shared, v_shared = kv[:, :, 0], kv[:, :, 1]
        else:
            j = i - N_A_LAYERS
            h = rmsnorm(x, b_norm[j])
            x = x + dilated_mixer(h, b_w_in[j], k_shared, v_shared, b_w_out[j])
    return rmsnorm(x, final_norm)


_drawn_inputs = setup_inputs


def setup_inputs(seed=0):
    import zlib

    import numpy as np

    out = dict(_drawn_inputs(seed))
    spreads = {}
    factors = {'a_g_out': 5.243, 'kv_norm': 8.0, 'b_norm': 8.0, 'final_norm': 2.889}
    for name, (base, spread) in spreads.items():
        noise = np.random.default_rng([zlib.crc32(name.encode()), seed]).standard_normal(out[name].shape)
        drawn = base * np.exp(spread * noise) if base else spread * noise
        out[name] = __import__('jax').numpy.asarray(drawn.astype(out[name].dtype))
    for name, factor in factors.items():
        out[name] = (out[name] * factor).astype(out[name].dtype)
    return out
```

```python
import concourse.bass as bass
from concourse import mybir
from contextlib import ExitStack

FP = mybir.dt.float32
FR = mybir.dt.float32r
I32 = mybir.dt.int32
ALU = mybir.AluOpType
ACT = mybir.ActivationFunctionType
AX = mybir.AxisListType

P = 128
SEQ, DM, DI = 512, 1024, 2048
NB = SEQ // P
KC = DM // P
EPS = 1e-6
GH, DV, RANK = 4, 512, 16
QK_SCALE = 128.0 ** -0.5
VCOL, ZCOL, LRCOL = DM, DM + DI, DM + 2 * DI
HEADS, GROUPS = 16, 3
UW = 256
UE = KC * UW
LEVELS = (64, 32, 16, 8, 4, 2, 1)
NL = len(LEVELS)
BATCHES = HEADS // 2
C_ID, C_TRI, C_DIST, C_MASK = 0, 128, 256, 768
C_SLOPE = C_MASK + 8 * 128
C_END = C_SLOPE + HEADS
G_A, G_KV, G_B, G_OUT = 0, 8, 16, 24

PJ_PRO, AT_PRO = ["A", None] * 2, ["D"] * 8 + ["A", "D"] + ["D"] * 4 + ["A"] * 4 + [None] * 2
PJ_HEAD, AT_HEAD = ["D"] * 8 + ["A", None] * 2 + ["D"] * 16 + [None] * 0, ["D"] * 18 + [None] * 2
PJ_LAST = ["D"] * 24
AT_MID = ["D"] * 8
PJ_FIRST, AT_FIRST = ["A"] * 18 + ["D"] * 2, ["D"] * 8
PJ_BATCH, AT_BATCH = ["A"] * 18 + ["D"] * 10, ["A", "D"] * 6 + ["D"] * 8
RSQ = 12


def adds(pj, at, tiles_of_units, **more):
    ends = [sum(tiles_of_units[:k + 1]) for k in range(len(tiles_of_units))]
    return dict(more, ends=ends, unit=len(ends), pj_slots=len(pj), at_slots=len(at),
                pj_full=len(pj) - pj.count(None), pj_fa=pj.count("A"), pj_fd=pj.count("D"),
                at_full=len(at) - at.count(None), at_fa=at.count("A"), at_fd=at.count("D"))


PER_HEAD = dict(dv=RSQ + 3, lvd=NL, lve=NL + 1, lvq=NL, bh=1, at_hi=2, ats=1, qd=1, sq=4, vh=4, th=4, oth=4)
PER_BATCH = dict(dv=9, zt=2, nb=1, ex=1, nrm=1)
PRO = adds(PJ_PRO, AT_PRO, [1, 1], dv=RSQ)
HEAD = adds(PJ_HEAD, AT_HEAD, [2, 2, 2, 2, 1, 1, 8, 8], **PER_HEAD)
LAST = adds(PJ_LAST, AT_HEAD, [2, 2, 2, 2, 8, 8], **PER_HEAD)
MID = adds([], AT_MID, [], dv=RSQ)
FIRST = adds(PJ_FIRST, AT_FIRST, [2] * 9 + [1, 1], **PER_BATCH)
BATCH = adds(PJ_BATCH, AT_BATCH, [2] * 9 + [1, 1, 8], og2=2, ob=2, ot2=2, **PER_BATCH)
TAIL = adds(["D"] * 8, AT_BATCH[:12], [8])


class Span:

    def __init__(self, before, per, turn=None):
        self.before, self.per, self.turn = before, per, turn

    def __call__(self, name, k):
        v = self.before.get(name, 0) + k
        return v if self.turn is None else self.turn * self.per.get(name, 0) + v

    def loads(self, k):
        v = 16 * ((self.before.get("unit", 0) + k) // 2 + 1)
        return v if self.turn is None else self.turn * (8 * self.per["unit"]) + v

    def parity(self, name, k, ring):
        assert self.turn is None or self.per.get(name, 0) % ring == 0
        return (self.before.get(name, 0) + k) % ring


def after(before, per, turns=1):
    names = (set(before) | set(per)) - {"ends"}
    return {k: before.get(k, 0) + turns * per.get(k, 0) for k in names}


B_PRO = {}
B_HEAD = after(B_PRO, PRO)
B_LAST = after(B_HEAD, HEAD, GH - 1)
B_MID = after(B_LAST, LAST)
B_FIRST = after(B_MID, MID)
B_BATCH = after(B_FIRST, FIRST)
B_FINAL = after(B_BATCH, BATCH, BATCHES - 2)
B_TAIL = after(B_FINAL, BATCH)


def trunk(nc, x, a_w_in, w_gate_up, a_w_out, w_kv, b_w_in, b_w_out, gains, final_norm, consts, out):
    ctx = ExitStack()
    with ctx:
        def sb(name, shape, dt=FP):
            return ctx.enter_context(nc.sbuf_tensor(name, shape, dt))

        def sem(name):
            return ctx.enter_context(nc.semaphore(name))

        cst = sb("cst", [P, C_END])
        gain = sb("gain", [P, 28])
        x1 = sb("x1", [P, NB, DM])
        big = sb("big", [P, NB, DM])
        hT = [sb(f"hT_{s}", [P, KC, SEQ], FR) for s in ("hi", "lo")]
        raw = [sb(f"raw{i}", [P, UE]) for i in range(2)]
        whi = [sb(f"whi{i}", [P, UE], FR) for i in range(2)]
        wlo = [sb(f"wlo{i}", [P, UE], FR) for i in range(2)]
        small = sb("small", [P, 96])
        ss, var, rstd, nwt = (small[:, 4 * i:4 * i + 4] for i in range(4))
        scr = sb("scr", [P, 2, 512])
        arena = sb("arena", [P, 13824])
        arena_r = sb("arena_r", [P, 11008], FR)

        def cut(t, at, *shape):
            n = 1
            for d in shape:
                n *= d
            v = t[:, at:at + n]
            if len(shape) == 2:
                v = v.rearrange("p (a b) -> p a b", a=shape[0])
            if len(shape) == 3:
                v = v.rearrange("p (a b c) -> p a b c", a=shape[0], b=shape[1])
            return v

        ident = cst[:, C_ID:C_ID + P]
        tri = cst[:, C_TRI:C_TRI + P]
        bT = cut(arena, 0, GH, SEQ)
        qk = cut(arena, 2048, 2, SEQ)
        ee = cut(arena, 3072, 2, SEQ)
        qkd = cut(arena, 4096, 2, 2, SEQ)
        atd = cut(arena, 6144, NB, P)
        e1 = cut(arena, 6656, 3, P)
        e2 = cut(arena, 7040, 3, P)
        qd = cut(arena, 7424, 4, P)
        kd = cut(arena, 7936, 4, P)
        gate = big[:, 0:2, :].rearrange("p a (b c) -> p (a b) c", b=2)
        lgate = big[:, 2:4, :].rearrange("p a (b c) -> p (a b) c", b=2)
        lr_n = arena[:, 8448:8512]
        lrT = arena[:, 8512:9024]
        wup = arena[:, 9024:9536]
        raw_lr = cut(arena, 9536, KC, RANK)
        etot = arena[:, 9664:9668]
        bh = arena[:, 9668:10180]
        tick = arena[:, 10180:10181]
        at = [cut(arena_r, 0, 10, P), cut(arena_r, 1280, 10, P)]
        lr_w = [cut(arena_r, 2560, KC, RANK), cut(arena_r, 2688, KC, RANK)]
        vr = [cut(arena_r, 6912, NB, DV), cut(arena_r, 8960, NB, DV)]
        oT = [cut(arena_r, 2816, NB, SEQ), cut(arena_r, 4864, NB, SEQ)]
        qT = [cut(arena, 1024 * i, 2, SEQ) for i in range(2)]
        kT = [cut(arena, 2048, 2, SEQ), big[:, 3, :].rearrange("p (j t) -> p j t", j=2)]
        vv = [cut(arena, 3072 + 1024 * g, NB, UW) for g in range(GROUPS)]
        s0 = cut(arena, 6144, 2, 896)
        s12 = [cut(arena, 7936 + 1024 * j, NB, 256) for j in range(2)]
        pT = cut(arena, 9984, 30, P)
        gate2 = big[:, 2, :].rearrange("p (j t) -> p j t", j=2)
        o_sum = big[:, 0, :].rearrange("p (j t) -> p j t", j=2)
        oT2 = [cut(arena_r, 0, 2, SEQ), cut(arena_r, 1024, 2, SEQ)]
        fnorm = big[:, 1, :]

        def stat(k):
            return small[:, 16 + 16 * k:32 + 16 * k].rearrange("p (l j b) -> p l j b", l=2, j=2)

        mx, nbias, lsum, rinv, xch = (stat(k) for k in range(5))
        PJ = [ctx.enter_context(nc.psum_tensor(f"PJ{i}", [P, 512], FP)) for i in range(4)]
        AT = [ctx.enter_context(nc.psum_tensor(f"AT{i}", [P, 512], FP)) for i in range(4)]

        raw_full = [sem("raw_full0"), sem("raw_full1")]
        hi_done, lo_done = sem("hi_done"), sem("lo_done")
        pj_full, pj_fa, pj_fd = sem("pj_full"), sem("pj_fa"), sem("pj_fd")
        at_full, at_fa, at_fd = sem("at_full"), sem("at_fa"), sem("at_fd")
        dv = sem("dv")
        x_in, x1_in, c_in, lr_in, fn_in = (sem(n) for n in ("x_in", "x1_in", "c_in", "lr_in", "fn_in"))
        sq_done, xn_done, ht_hi = sem("sq_done"), sem("xn_done"), sem("ht_hi")
        lr_hi, lr_split, ones_set = sem("lr_hi"), sem("lr_split"), sem("ones_set")
        u_abs, u_exp, u_ln = sem("u_abs"), sem("u_exp"), sem("u_ln")
        y_done, out_done = sem("y_done"), sem("out_done")
        bh_done, lvd, lve, lvq, at_hi, ats = (sem(n) for n in ("bh_done", "lvd", "lve", "lvq", "at_hi", "ats"))
        qd_done, head_sq, vh, th, oth = (sem(n) for n in ("qd_done", "head_sq", "vh", "th", "oth"))
        nb_done, ex_done, nrm_done, zt = (sem(n) for n in ("nb_done", "ex_done", "nrm_done", "zt"))
        og2, ob, ot2 = (sem(n) for n in ("og2", "ob", "ot2"))

        def by_rows(w):
            return w.rearrange("(k p) c -> p k c", p=P)

        w_a, w_b, w_s = by_rows(a_w_in), by_rows(b_w_in), by_rows(w_kv)
        o_a, o_b = by_rows(a_w_out), by_rows(b_w_out)

        def in_unit(w, col, cols, g):
            return (w[:, :, bass.ds(col, cols)], KC, cols, g)

        def out_unit(w, row, g):
            return (w[:, bass.ds(row, 2), :], 2, DM, g)

        def v_a(h, u):
            return in_unit(w_a, h * DV + (VCOL + u * UW), UW, G_A)

        def z_a(h, u):
            return in_unit(w_a, h * DV + (ZCOL + u * UW), UW, G_A)

        def qk_a(h, i):
            return in_unit(w_a, h * P + i * GH * P, P, G_A)

        def head_units(h, last):
            mid = [] if last else [qk_a(h + 1, 0), qk_a(h + 1, 1)]
            return ([v_a(h, 0), v_a(h, 1), z_a(h, 0), z_a(h, 1)] + mid
                    + [out_unit(o_a, h * 4 + 2 * u, G_OUT + 2 * u) for u in range(2)])

        def batch_units(n, first):
            u = []
            for g in range(GROUPS):
                u += [in_unit(w_b, n * UW + g * DI, UW, G_B), in_unit(w_s, n * UW + g * DI, UW, G_KV)]
            u += [in_unit(w_s, n * UW + (GROUPS + g) * DI, UW, G_KV) for g in range(GROUPS)]
            u += [in_unit(w_b, n * UW + (GROUPS * DI + j * P), P, G_B) for j in range(2)]
            return u if first else u + [out_unit(o_b, n * 2 + (-2), None)]

        FIRST_QK = [qk_a(0, 0), qk_a(0, 1)]
        LAST_OUT = out_unit(o_b, HEADS - 2, None)

        def unit_view(t, unit):
            _, k, cols, _ = unit
            return t[:, 0:k * cols].rearrange("p (k c) -> p k c", k=k)

        def turns(eng, lo, hi, before, per, body):
            with eng.Fori(0, hi - lo) as i:
                body(i + lo, Span(before, per, i))

        block = ctx.enter_context(nc.Block())

        @block.sync
        def _(sp):
            def load(c, k, unit):
                u = c("unit", k)
                slot = c.parity("unit", k, 2)
                if not isinstance(u, int) or u >= 2:
                    sp.wait_ge(lo_done, c("unit", k - 1))
                sp.dma_start(unit_view(raw[slot], unit), unit[0]).then_inc(raw_full[slot], 16)

            sp.dma_start(cst[:, :], consts).then_inc(c_in, 16)
            for b in range(NB):
                sp.dma_start(big[:, b, :], x[b * P:(b + 1) * P, :]).then_inc(x_in, 16)
            c = Span(B_PRO, PRO)
            for k, unit in enumerate(FIRST_QK):
                load(c, k, unit)

            def head(h, c, last=False):
                for k, unit in enumerate(head_units(h, last)):
                    load(c, k, unit)

            turns(sp, 0, GH - 1, B_HEAD, HEAD, head)
            head(GH - 1, Span(B_LAST, LAST), True)

            def batch(n, c, first=False):
                for k, unit in enumerate(batch_units(n, first)):
                    load(c, k, unit)

            batch(0, Span(B_FIRST, FIRST), True)
            turns(sp, 1, BATCHES - 1, B_BATCH, BATCH, batch)
            batch(BATCHES - 1, Span(B_FINAL, BATCH))
            load(Span(B_TAIL, TAIL), 0, LAST_OUT)
            sp.wait_ge(at_fd, B_FIRST["at_fd"])
            sp.dma_start(fnorm, final_norm.rearrange("(a n) -> a n", a=1).to_broadcast([P, DM])).then_inc(fn_in, 16)
            for b in range(NB):
                sp.wait_ge(y_done, b + 1)
                sp.dma_start(out[b * P:(b + 1) * P, :], x1[:, b, :]).then_inc(out_done, 16)
            sp.wait_ge(out_done, 64)

        @block.gpsimd
        def _(pool):
            pool.memset(lrT[0:32, :], 1.0).then_inc(ones_set, 1)

            def head(h, c):
                pool.wait_ge(bh_done, c("bh", 1))
                for i, L in enumerate(LEVELS):
                    v = bh[:, :].rearrange("p (n u l) -> p n u l", u=2, l=L)
                    d = ee[:, i % 2, :].rearrange("p (n u l) -> p n u l", u=2, l=L)
                    ref = v[:, :, 0, L - 1:L].to_broadcast([P, SEQ // (2 * L), L])
                    w = c("lvq", max(i - 1, 0))
                    if not isinstance(w, int) or w:
                        pool.wait_ge(lvq, w)
                    pool.tensor_tensor(d[:, :, 0, :], ref, v[:, :, 0, :], ALU.subtract)
                    pool.tensor_tensor(d[:, :, 1, :], v[:, :, 1, :], ref, ALU.subtract).then_inc(lvd, 1)

            turns(pool, 0, GH - 1, B_HEAD, HEAD, head)
            head(GH - 1, Span(B_LAST, LAST))

        @block.scalar
        def _(act):
            def hi(c, k, unit):
                slot = c.parity("unit", k, 2)
                u = c("unit", k)
                act.wait_ge(raw_full[slot], c.loads(k))
                if not isinstance(u, int) or u >= 2:
                    act.wait_ge(pj_full, c("pj_full", c.per["ends"][k - 2] if k >= 2 else 0))
                src, dst = unit_view(raw[slot], unit), unit_view(whi[slot], unit)
                if unit[3] is None:
                    nc.scalar.activation(dst, src, ACT.Copy).then_inc(hi_done, 1)
                    return
                for j in range(unit[1]):
                    ins = nc.scalar.activation(dst[:, j, :], src[:, j, :], ACT.Copy,
                                               scale=gain[:, unit[3] + j:unit[3] + j + 1])
                ins.then_inc(hi_done, 1)

            def squares(src, done):
                for b in range(NB):
                    if b:
                        act.wait_ge(sq_done, done + b)
                    nc.scalar.activation(scr[:, :, :].rearrange("p a b -> p (a b)"), src[:, b, :], ACT.Square,
                                         accum_out=ss[:, b:b + 1]).then_inc(sq_done, 1)

            def transposed(c, done):
                for k in range(KC):
                    act.wait_ge(at_full, c("at_full", k + 1))
                    nc.scalar.activation(hT[0][:, k, :], AT[c.parity("at_slots", k, 4)][:, :],
                                         ACT.Copy).then_inc(ht_hi, 1)

            act.dma_start(gain[:, :], gains).then_inc(lr_in, 16)
            act.dma_start(raw_lr[:, :, :], w_a[:, :, LRCOL:LRCOL + RANK]).then_inc(lr_in, 16)
            act.dma_start(wup[0:RANK + 1, :], w_gate_up).then_inc(lr_in, 16)
            act.dma_start(x1[:, :, :], x.rearrange("(b p) d -> p b d", p=P)).then_inc(x1_in, 16)
            c = Span(B_PRO, PRO)
            act.wait_ge(x_in, 16 * NB)
            squares(big, 0)
            act.wait_ge(lr_in, 48)
            for j in range(KC):
                ins = nc.scalar.activation(lr_w[0][:, j, :], raw_lr[:, j, :], ACT.Copy, scale=gain[:, j:j + 1])
            ins.then_inc(lr_hi, 1)
            hi(c, 0, FIRST_QK[0])
            transposed(c, 0)
            hi(c, 1, FIRST_QK[1])
            act.wait_ge(at_full, KC + 1)
            nc.scalar.activation(lr_n, AT[0][:, 0:64], ACT.Copy).then_inc(at_fa, 1)
            for b in range(NB):
                act.wait_ge(at_full, KC + 3 + b)
                nc.scalar.activation(scr[:, b % 2, :], AT[(KC + 2 + b) % 4][:, :], ACT.Abs).then_inc(u_abs, 1)
                act.wait_ge(u_abs, b + 1)
                nc.scalar.activation(gate[:, b, :], scr[:, b % 2, :], ACT.Exp, scale=-1.0).then_inc(u_exp, 1)
            for b in range(NB):
                act.wait_ge(u_exp, b + 1)
                nc.scalar.activation(lgate[:, b, :], gate[:, b, :], ACT.Ln, bias=1.0).then_inc(u_ln, 1)
            for h in range(GH):
                act.wait_ge(at_full, KC + 7 + h)
                nc.scalar.activation(bT[:, h, :], AT[(KC + 6 + h) % 4][:, :], ACT.Copy).then_inc(at_fa, 1)

            def q_or_k(c, i, tile, pj_index):
                act.wait_ge(pj_full, c("pj_full", pj_index + 1))
                nc.scalar.activation(qk[:, i, :], PJ[tile % 4][:, :], ACT.Copy,
                                     scale=QK_SCALE if i == 0 else 1.0).then_inc(pj_fa, 1)

            for i in range(2):
                q_or_k(c, i, 2 * i, i)

            def head(h, c, last=False, nxt=None):
                units = head_units(h, last) + [nxt(h)]
                b = bh[:, :].rearrange("p (n t) -> p n t", t=P)

                def value_hi(u):
                    for i in range(2):
                        t = 2 * u + i
                        act.wait_ge(pj_full, c("pj_full", t + 1))
                        nc.scalar.activation(vr[0][:, 2 * i:2 * i + 2, u * UW:(u + 1) * UW],
                                             PJ[t % 4][:, :].rearrange("p (s c) -> p s c", s=2),
                                             ACT.Copy).then_inc(vh, 1)

                def tanh(u):
                    for i in range(2):
                        t = 4 + 2 * u + i
                        act.wait_ge(pj_full, c("pj_full", t + 1))
                        act.wait_ge(pj_fd, c("pj_fd", t - 2))
                        nc.scalar.activation(scr[:, i, :], PJ[t % 4][:, :], ACT.Tanh, scale=0.5).then_inc(th, 1)

                def exps(lo, up):
                    for i in range(lo, up):
                        act.wait_ge(lvd, c("lvd", i + 1))
                        nc.scalar.activation(ee[:, i % 2, :], ee[:, i % 2, :], ACT.Exp).then_inc(lve, 1)

                act.wait_ge(at_fa, c("at_fa", 0))
                w = c("lvq", 0)
                if not isinstance(w, int) or w:
                    act.wait_ge(lvd, c("lvd", 0))
                nc.scalar.activation(bh[:, :].unsqueeze(1), bT[:, bass.ds(h, 1), :], ACT.Copy).then_inc(bh_done, 1)
                hi(c, 1, units[1])
                exps(0, 3)
                value_hi(0)
                hi(c, 2, units[2])
                exps(3, 6)
                nc.scalar.activation(e1[:, :, :], b[:, 1:4, :], ACT.Exp)
                nc.scalar.activation(etot, b[:, :, P - 1], ACT.Exp)
                for s in range(3):
                    ins = nc.scalar.activation(e2[:, s, :], b[:, s, :], ACT.Exp, scale=-1.0, bias=b[:, s, P - 1:P])
                ins.then_inc(lve, 1)
                value_hi(1)
                hi(c, 3, units[3])
                act.wait_ge(lvd, c("lvd", NL))
                nc.scalar.activation(ee[:, (NL - 1) % 2, :], ee[:, (NL - 1) % 2, :], ACT.Exp).then_inc(lve, 1)
                tanh(0)
                act.wait_ge(at_fd, c("at_fd", NL + 1))
                nc.scalar.activation(at[0][:, 0:4, :], atd[:, :, :], ACT.Copy).then_inc(at_hi, 1)
                for i in range(2):
                    act.wait_ge(at_full, c("at_full", NL + 2 + i))
                    ins = nc.scalar.activation(at[0][:, 4 + 3 * i:7 + 3 * i, :].rearrange("p a b -> p (a b)"),
                                               AT[c.parity("at_slots", NL + 1 + i, 4)][:, 0:384], ACT.Copy)
                ins.then_inc(at_hi, 1)
                hi(c, 4, units[4])
                tanh(1)
                act.wait_ge(pj_fd, c("pj_fd", 8))
                for i in range(NB):
                    act.wait_ge(at_full, c("at_full", NL + 4 + i))
                    if i >= 2:
                        act.wait_ge(head_sq, c("sq", i - 1))
                    nc.scalar.activation(scr[:, i % 2, :], AT[c.parity("at_slots", NL + 3 + i, 4)][:, :],
                                         ACT.Square, accum_out=ss[:, i:i + 1]).then_inc(head_sq, 1)
                hi(c, 5, units[5])
                if not last:
                    act.wait_ge(qd_done, c("qd", 1))
                    q_or_k(c, 0, 8, 8)
                    hi(c, 6, units[6])
                    q_or_k(c, 1, 10, 9)
                for i in range(4):
                    act.wait_ge(at_full, c("at_full", NL + 8 + i))
                    nc.scalar.activation(oT[0][:, i, :], AT[c.parity("at_slots", NL + 7 + i, 4)][:, :],
                                         ACT.Copy).then_inc(oth, 1)
                for k in range(6 if last else 7, len(units)):
                    hi(c, k, units[k])

            hi(c, 2, v_a(0, 0))
            turns(act, 0, GH - 1, B_HEAD, HEAD, lambda h, c: head(h, c, nxt=lambda h: v_a(h + 1, 0)))
            head(GH - 1, Span(B_LAST, LAST), True, nxt=lambda h: batch_units(0, True)[0])

            c = Span(B_MID, MID)
            act.wait_ge(pj_fd, c("pj_fd", 0))
            squares(x1, NB)
            transposed(c, KC)

            def batch(n, c, first=False, nxt=None):
                units = batch_units(n, first) + [nxt]

                def copy(tile, dst, src=None):
                    act.wait_ge(pj_full, c("pj_full", tile + 1))
                    bank = PJ[tile % 4][:, :]
                    nc.scalar.activation(dst, bank if src is None else src(bank), ACT.Copy).then_inc(pj_fa, 1)

                def heads(tile, dst, order):
                    for j in range(2):
                        if order == "tokens":
                            copy(tile + j, dst[:, j, :])
                        elif order == "blocks":
                            copy(tile + j, dst[:, j, :].rearrange("p (b r i) -> p b r i", b=NB, r=4),
                                 lambda t: t.rearrange("p (b i r) -> p b r i", b=NB, r=4))
                        else:
                            copy(tile + j, dst[:, j, :].rearrange("p (r j) -> p r j", r=4),
                                 lambda t: t.rearrange("p (j r) -> p r j", r=4))

                def values(g):
                    for i in range(2):
                        copy(12 + 2 * g + i, vv[g][:, 2 * i:2 * i + 2, :],
                             lambda t: t.rearrange("p (s c) -> p s c", s=2))

                hi(c, 1, units[1])
                if not first:
                    for t in range(0, 8, 2):
                        act.wait_ge(at_full, c("at_full", t + 1))
                        nc.scalar.activation(pT[:, 4 * t:4 * t + 4, :].rearrange("p a b -> p (a b)"),
                                             AT[c.parity("at_slots", t, 4)][:, :], ACT.Copy).then_inc(at_fa, 1)
                heads(0, qT[0], "blocks")
                hi(c, 2, units[2])
                heads(2, kT[0], "tokens")
                if not first:
                    attended_act(c)
                hi(c, 3, units[3])
                heads(4, qT[1], "classes")
                hi(c, 4, units[4])
                heads(6, kT[1], "classes")
                hi(c, 5, units[5])
                heads(8, qT[0], "classes")
                hi(c, 6, units[6])
                heads(10, kT[0], "classes")
                hi(c, 7, units[7])
                values(0)
                hi(c, 8, units[8])
                values(1)
                hi(c, 9, units[9])
                values(2)
                hi(c, 10, units[10])
                act.wait_ge(nb_done, c("nb", 1))
                for j in range(2):
                    for b in range(NB):
                        w = slice(max(256 * b - 128, 0), 256 * b + 128)
                        nc.scalar.activation(s0[:, j, w], s0[:, j, w], ACT.Exp, scale=QK_SCALE,
                                             bias=nbias[:, 0, j, b:b + 1], accum_out=lsum[:, 0, j, b:b + 1])
                        ins = nc.scalar.activation(s12[j][:, b, :], s12[j][:, b, :], ACT.Exp, scale=QK_SCALE,
                                                   bias=nbias[:, 1, j, b:b + 1], accum_out=lsum[:, 1, j, b:b + 1])
                ins.then_inc(ex_done, 1)
                for j in range(2):
                    act.wait_ge(pj_full, c("pj_full", 19 + j))
                    nc.scalar.activation(scr[:, j, :], PJ[(18 + j) % 4][:, :], ACT.Tanh, scale=0.5).then_inc(zt, 1)
                    if j == 0 and not first:
                        hi(c, 11, units[11])
                hi(c, len(units) - 1, units[-1])

            def attended_act(c):
                for j in range(2):
                    act.wait_ge(at_full, c("at_full", 9 + 2 * j))
                    nc.scalar.activation(o_sum[:, j, :].rearrange("p (b i r) -> p b r i", b=NB, r=4),
                                         AT[c.parity("at_slots", 8 + 2 * j, 4)][:, :].rearrange(
                                             "p (b r i) -> p b r i", b=NB, r=4), ACT.Copy).then_inc(at_fa, 1)
                for j in range(2):
                    act.wait_ge(og2, c("og2", j + 1))
                    nc.scalar.activation(oT2[0][:, j, :], o_sum[:, j, :], ACT.Copy).then_inc(ob, 1)

            batch(0, Span(B_FIRST, FIRST), True, batch_units(1, False)[0])
            turns(act, 1, BATCHES - 1, B_BATCH, BATCH,
                  lambda n, c: batch(n, c, nxt=batch_units(n + 1, False)[0]))
            batch(BATCHES - 1, Span(B_FINAL, BATCH), nxt=LAST_OUT)
            c = Span(B_TAIL, TAIL)
            for t in range(0, 8, 2):
                act.wait_ge(at_full, c("at_full", t + 1))
                nc.scalar.activation(pT[:, 4 * t:4 * t + 4, :].rearrange("p a b -> p (a b)"),
                                     AT[c.parity("at_slots", t, 4)][:, :], ACT.Copy).then_inc(at_fa, 1)
            attended_act(c)
            act.wait_ge(pj_fd, c("pj_fd", 8))
            squares(x1, 2 * NB)

        @block.vector
        def _(dve):
            def link(c, k, ins):
                ins.then_inc(dv, 1)
                dve.wait_ge(dv, c("dv", k + 1))

            def lo(c, k, unit):
                slot = c.parity("unit", k, 2)
                dve.wait_ge(hi_done, c("unit", k + 1))
                src, h, dst = (unit_view(t[slot], unit) for t in (raw, whi, wlo))
                h = h.bitcast(FP)
                if unit[3] is None:
                    nc.vector.tensor_tensor(dst, src, h, ALU.subtract).then_inc(lo_done, 1)
                    return
                for j in range(unit[1]):
                    ins = nc.vector.scalar_tensor_tensor(out=dst[:, j, :], in0=src[:, j, :],
                                                         scalar=gain[:, unit[3] + j:unit[3] + j + 1],
                                                         in1=h[:, j, :], op0=ALU.mult, op1=ALU.subtract)
                ins.then_inc(lo_done, 1)

            def inverse_root(c, k, width):
                v = nc.vector
                link(c, k, v.tensor_scalar(var, ss, 1.0 / width, EPS, ALU.mult, ALU.add))
                link(c, k + 1, v.tensor_scalar(rstd.bitcast(I32), var.bitcast(I32), 1, None, ALU.logical_shift_right))
                link(c, k + 2, v.tensor_scalar(rstd.bitcast(I32), rstd.bitcast(I32), -1.0, float(0x5F3759DF),
                                               ALU.mult, ALU.add))
                for i in range(3):
                    link(c, k + 3 + 3 * i, v.tensor_tensor(nwt, rstd, rstd, ALU.mult))
                    link(c, k + 4 + 3 * i, v.scalar_tensor_tensor(out=nwt, in0=nwt, scalar=-0.5, in1=var,
                                                                  op0=ALU.mult, op1=ALU.mult))
                    last = v.scalar_tensor_tensor(out=rstd, in0=nwt, scalar=1.5, in1=rstd, op0=ALU.add, op1=ALU.mult)
                    link(c, k + 5 + 3 * i, last)

            def transposed_lo(c, done):
                for k in range(KC):
                    dve.wait_ge(ht_hi, done + k + 1)
                    nc.vector.tensor_tensor(hT[1][:, k, :], AT[c.parity("at_slots", k, 4)][:, :],
                                            hT[0][:, k, :].bitcast(FP), ALU.subtract).then_inc(at_fd, 1)

            c = Span(B_PRO, PRO)
            dve.wait_ge(sq_done, NB)
            inverse_root(c, 0, DM)
            for b in range(NB):
                nc.vector.tensor_scalar(big[:, b, :], big[:, b, :], rstd[:, b:b + 1], None, ALU.mult).then_inc(xn_done, 1)
            dve.wait_ge(lr_hi, 1)
            for j in range(KC):
                ins = nc.vector.scalar_tensor_tensor(out=lr_w[1][:, j, :], in0=raw_lr[:, j, :], scalar=gain[:, j:j + 1],
                                                     in1=lr_w[0].bitcast(FP)[:, j, :], op0=ALU.mult, op1=ALU.subtract)
            ins.then_inc(lr_split, 1)
            lo(c, 0, FIRST_QK[0])
            transposed_lo(c, 0)
            lo(c, 1, FIRST_QK[1])
            dve.wait_ge(at_full, KC + 2)
            dve.wait_ge(ones_set, 1)
            nc.vector.tensor_copy(lrT[0:RANK, :], AT[(KC + 1) % 4][0:RANK, :]).then_inc(at_fd, 1)
            for b in range(NB):
                dve.wait_ge(u_ln, b + 1)
                nc.vector.scalar_tensor_tensor(out=lgate[:, b, :], in0=AT[(KC + 2 + b) % 4][:, :], scalar=0.0,
                                               in1=lgate[:, b, :], op0=ALU.min, op1=ALU.subtract).then_inc(at_fd, 1)

            def add_out(c, tile, count):
                for t in range(8):
                    dve.wait_ge(pj_full, c("pj_full", count + t + 1))
                    o = x1[:, t // 2, (t % 2) * 512:(t % 2) * 512 + 512]
                    nc.vector.tensor_tensor(o, PJ[(tile + t) % 4][:, :], o, ALU.add).then_inc(pj_fd, 1)

            def head(h, c, last=False, nxt=None):
                units = head_units(h, last) + [nxt(h)]

                def value_lo(u):
                    for i in range(2):
                        t = 2 * u + i
                        dve.wait_ge(vh, c("vh", t + 1))
                        w = (slice(None), slice(2 * i, 2 * i + 2), slice(u * UW, (u + 1) * UW))
                        nc.vector.tensor_tensor(vr[1][w], PJ[t % 4][:, :].rearrange("p (s c) -> p s c", s=2),
                                                vr[0].bitcast(FP)[w], ALU.subtract).then_inc(pj_fd, 1)

                def gates(u):
                    for i in range(2):
                        t = 4 + 2 * u + i
                        dve.wait_ge(th, c("th", 2 * u + i + 1))
                        nc.vector.scalar_tensor_tensor(
                            out=gate[:, 2 * i:2 * i + 2, u * UW:(u + 1) * UW],
                            in0=scr[:, i, :].rearrange("p (s c) -> p s c", s=2), scalar=1.0,
                            in1=PJ[t % 4][:, :].rearrange("p (s c) -> p s c", s=2),
                            op0=ALU.add, op1=ALU.mult).then_inc(pj_fd, 1)

                def decay(i):
                    dve.wait_ge(lve, c("lve", i + 1 + (i == NL - 1)))
                    w = max(i - 1, 0)
                    dve.wait_ge(at_full, c("at_full", w))
                    nc.vector.tensor_tensor(qkd[:, i % 2, :, :], qk[:, :, :],
                                            ee[:, i % 2, :].unsqueeze(1).to_broadcast([P, 2, SEQ]),
                                            ALU.mult).then_inc(lvq, 1)

                def keep(i):
                    dve.wait_ge(at_full, c("at_full", i + 1))
                    if i == 0:
                        dve.wait_ge(dv, c("dv", 1))
                    else:
                        dve.wait_ge(at_fd, c("at_fd", i))
                    nc.vector.memset(tick, 0.0)
                    m = cst[:, C_MASK + i * P:C_MASK + (i + 1) * P].bitcast(I32)
                    nc.vector.copy_predicated(atd[:, :, :], m.unsqueeze(1).to_broadcast([P, NB, P]),
                                              AT[c.parity("at_slots", i, 4)][:, :].rearrange("p (b t) -> p b t", b=NB))\
                        .then_inc(at_fd, 1)

                lo(c, 1, units[1])
                nc.vector.memset(atd[:, :, :], 0.0).then_inc(dv, 1)
                dve.wait_ge(pj_fa, c("pj_fa", 0))
                decay(0)
                decay(1)
                value_lo(0)
                keep(0)
                decay(2)
                keep(1)
                lo(c, 2, units[2])
                keep(2)
                decay(3)
                decay(4)
                value_lo(1)
                keep(3)
                decay(5)
                keep(4)
                lo(c, 3, units[3])
                keep(5)
                decay(6)
                q4, k4 = (qk[:, i, :].rearrange("p (b t) -> p b t", b=NB) for i in range(2))
                v = nc.vector
                v.tensor_tensor(qd[:, 0:2, :], q4[:, 1:3, :], e1[:, 0:2, :], ALU.mult)
                v.tensor_tensor(qd[:, 3, :], q4[:, 3, :], e1[:, 2, :], ALU.mult)
                link(c, 1, v.tensor_tensor(kd[:, 0:3, :], k4[:, 0:3, :], e2[:, :, :], ALU.mult))
                v.tensor_scalar(qd[:, 2, :], qd[:, 3, :], etot[:, 2:3], None, ALU.mult)
                v.tensor_scalar(kd[:, 3, :], kd[:, 0, :], etot[:, 1:2], None, ALU.mult).then_inc(qd_done, 1)
                gates(0)
                keep(6)
                keep(7)
                dve.wait_ge(at_fd, c("at_fd", NL + 1))
                dve.wait_ge(at_hi, c("at_hi", 1))
                nc.vector.tensor_tensor(at[1][:, 0:4, :], atd[:, :, :], at[0][:, 0:4, :].bitcast(FP),
                                        ALU.subtract).then_inc(ats, 1)
                dve.wait_ge(at_hi, c("at_hi", 2))
                for i in range(2):
                    w = slice(4 + 3 * i, 7 + 3 * i)
                    nc.vector.tensor_tensor(at[1][:, w, :].rearrange("p a b -> p (a b)"),
                                            AT[c.parity("at_slots", NL + 1 + i, 4)][:, 0:384],
                                            at[0][:, w, :].bitcast(FP).rearrange("p a b -> p (a b)"),
                                            ALU.subtract).then_inc(at_fd, 1)
                lo(c, 4, units[4])
                gates(1)
                dve.wait_ge(head_sq, c("sq", 4))
                dve.wait_ge(pj_fd, c("pj_fd", 8))
                inverse_root(c, 2, DV)
                link(c, 2 + RSQ, v.tensor_scalar(rstd, rstd, 0.5, None, ALU.mult))
                for i in range(NB):
                    ins = nc.vector.scalar_tensor_tensor(out=gate[:, i, :], in0=AT[c.parity("at_slots", NL + 3 + i, 4)][:, :],
                                                         scalar=rstd[:, i:i + 1], in1=gate[:, i, :],
                                                         op0=ALU.mult, op1=ALU.mult)
                    ins.then_inc(at_fd, 1)
                lo(c, 5, units[5])
                if not last:
                    lo(c, 6, units[6])
                for i in range(4):
                    dve.wait_ge(oth, c("oth", i + 1))
                    nc.vector.tensor_tensor(oT[1][:, i, :], AT[c.parity("at_slots", NL + 7 + i, 4)][:, :],
                                            oT[0].bitcast(FP)[:, i, :], ALU.subtract).then_inc(at_fd, 1)
                tile, count = (8, 8) if last else (12, 10)
                if last:
                    add_out(c, tile, count)
                    lo(c, 6, units[6])
                    add_out(c, tile + 8, count + 8)
                else:
                    lo(c, 7, units[7])
                    add_out(c, tile, count)
                    lo(c, 8, units[8])
                    add_out(c, tile + 8, count + 8)

            lo(c, 2, v_a(0, 0))
            dve.wait_ge(x1_in, 16)
            turns(dve, 0, GH - 1, B_HEAD, HEAD, lambda h, c: head(h, c, nxt=lambda h: v_a(h + 1, 0)))
            head(GH - 1, Span(B_LAST, LAST), True, nxt=lambda h: batch_units(0, True)[0])

            c = Span(B_MID, MID)
            dve.wait_ge(sq_done, 2 * NB)
            inverse_root(c, 0, DM)
            for b in range(NB):
                nc.vector.tensor_scalar(big[:, b, :], x1[:, b, :], rstd[:, b:b + 1], None, ALU.mult).then_inc(xn_done, 1)
            transposed_lo(c, KC)

            def swap(c, k, dst, src):
                for a in range(4):
                    for b in range(4):
                        ins = nc.vector.tensor_copy(dst[32 * a:32 * a + 32, :, b], src[32 * b:32 * b + 32, :, a])
                link(c, k, ins)

            def attended(c):
                for j in range(2):
                    dve.wait_ge(at_fa, c("at_fa", 5 + j))
                    dve.wait_ge(at_full, c("at_full", 10 + 2 * j))
                    o = o_sum[:, j, :]
                    by_class = o.rearrange("p (j r) -> p r j", r=4)
                    nc.vector.tensor_tensor(by_class, AT[c.parity("at_slots", 9 + 2 * j, 4)][:, :].rearrange(
                        "p (r j) -> p r j", r=4), by_class, ALU.add).then_inc(at_fd, 1)
                    dve.wait_ge(at_fd, c("at_fd", 5 + j))
                    nc.vector.tensor_tensor(o, o, gate2[:, j, :], ALU.mult).then_inc(og2, 1)
                for j in range(2):
                    dve.wait_ge(ob, c("ob", j + 1))
                    ins = nc.vector.tensor_tensor(oT2[1][:, j, :], o_sum[:, j, :], oT2[0][:, j, :].bitcast(FP),
                                                  ALU.subtract)
                    ins.then_inc(ot2, 1)

            def batch(n, c, first=False, nxt=None):
                units = batch_units(n, first) + [nxt]
                a0 = 0 if first else 12

                def bias0():
                    for j in range(2):
                        sl = slopes(n, j)
                        t0, t1 = (AT[c.parity("at_slots", a0 + 2 * j + i, 4)] for i in range(2))
                        d = cst[:, C_DIST:C_DIST + 256]
                        dve.wait_ge(at_full, c("at_full", a0 + 2 * j + 1))
                        nc.vector.scalar_tensor_tensor(out=s0[:, j, 0:128], in0=d[:, 128:256], scalar=sl,
                                                       in1=t0[:, 0:128], op0=ALU.mult, op1=ALU.add)
                        nc.vector.scalar_tensor_tensor(out=s0[:, j, 128:384], in0=d, scalar=sl,
                                                       in1=t0[:, 128:384], op0=ALU.mult, op1=ALU.add).then_inc(at_fd, 1)
                        dve.wait_ge(at_full, c("at_full", a0 + 2 * j + 2))
                        nc.vector.scalar_tensor_tensor(
                            out=s0[:, j, 384:896].rearrange("p (a k) -> p a k", a=2),
                            in0=d.unsqueeze(1).to_broadcast([P, 2, 256]), scalar=sl,
                            in1=t1[:, :].rearrange("p (a k) -> p a k", a=2), op0=ALU.mult, op1=ALU.add).then_inc(at_fd, 1)

                def bias12(g):
                    for j in range(2):
                        t = a0 + 4 + 2 * (g - 1) + j
                        d = cst[:, C_DIST + 128 + 128 * g:C_DIST + 256 + 128 * g]
                        dve.wait_ge(at_full, c("at_full", t + 1))
                        nc.vector.scalar_tensor_tensor(
                            out=s12[j][:, :, 128 * (g - 1):128 * g], in0=d.unsqueeze(1).to_broadcast([P, 4, 128]),
                            scalar=slopes(n, j), in1=AT[c.parity("at_slots", t, 4)][:, :].rearrange("p (r k) -> p r k", r=4),
                            op0=ALU.mult, op1=ALU.add).then_inc(at_fd, 1)

                lo(c, 1, units[1])
                if not first:
                    probs_out(c)
                lo(c, 2, units[2])
                if not first:
                    attended(c)
                lo(c, 3, units[3])
                bias0()
                lo(c, 4, units[4])
                lo(c, 5, units[5])
                bias12(1)
                lo(c, 6, units[6])
                lo(c, 7, units[7])
                bias12(2)
                dve.wait_ge(at_fd, c("at_fd", 8 if first else 14))
                v = nc.vector
                for j in range(2):
                    v.tensor_reduce(mx[:, 0, j, 0:1], s0[:, j, 0:128], AX.X, ALU.max)
                    v.tensor_reduce(mx[:, 0, j, 1:4], s0[:, j, 128:896].rearrange("p (b k) -> p b k", b=3), AX.X, ALU.max)
                    ins = v.tensor_reduce(mx[:, 1, j, :], s12[j][:, :, :], AX.X, ALU.max)
                link(c, 0, ins)
                swap(c, 1, xch[:, 0], mx[:, 1])
                link(c, 2, v.tensor_tensor(mx[:, 0], mx[:, 0], xch[:, 0], ALU.max))
                swap(c, 3, mx[:, 1], mx[:, 0])
                v.tensor_scalar(nbias[:, :, :, :], mx[:, :, :, :], -QK_SCALE, None, ALU.mult).then_inc(nb_done, 1)
                lo(c, 8, units[8])
                lo(c, 9, units[9])
                lo(c, 10, units[10])
                dve.wait_ge(ex_done, c("ex", 1))
                swap(c, 4, xch[:, 0], lsum[:, 1])
                link(c, 5, v.tensor_tensor(lsum[:, 0], lsum[:, 0], xch[:, 0], ALU.add))
                swap(c, 6, lsum[:, 1], lsum[:, 0])
                link(c, 7, v.tensor_scalar(lsum[:, :, :, :], lsum[:, :, :, :], 2.0, None, ALU.mult))
                link(c, 8, v.reciprocal(rinv[:, :, :, :], lsum[:, :, :, :]))
                for j in range(2):
                    for b in range(NB):
                        w = slice(max(256 * b - 128, 0), 256 * b + 128)
                        v.tensor_scalar(s0[:, j, w], s0[:, j, w], rinv[:, 0, j, b:b + 1], None, ALU.mult)
                        ins = v.tensor_scalar(s12[j][:, b, :], s12[j][:, b, :], rinv[:, 1, j, b:b + 1], None, ALU.mult)
                ins.then_inc(nrm_done, 1)
                for j in range(2):
                    dve.wait_ge(zt, c("zt", j + 1))
                    v.scalar_tensor_tensor(out=gate2[:, j, :], in0=scr[:, j, :], scalar=1.0, in1=PJ[(18 + j) % 4][:, :],
                                           op0=ALU.add, op1=ALU.mult).then_inc(pj_fd, 1)
                    if j == 0 and not first:
                        lo(c, 11, units[11])
                lo(c, len(units) - 1, units[-1])
                if not first:
                    add_out(c, 20, 20)

            def slopes(n, j):
                return cst[:, bass.ds(n * 2 + (C_SLOPE + j), 1)]

            def probs_out(c):
                for t in range(1, 8, 2):
                    w = 512 if t < 7 else 256
                    dve.wait_ge(at_full, c("at_full", t + 1))
                    nc.vector.tensor_copy(pT[:, 4 * t:4 * t + w // P, :].rearrange("p a b -> p (a b)"),
                                          AT[c.parity("at_slots", t, 4)][:, 0:w]).then_inc(at_fd, 1)

            batch(0, Span(B_FIRST, FIRST), True, batch_units(1, False)[0])
            turns(dve, 1, BATCHES - 1, B_BATCH, BATCH,
                  lambda n, c: batch(n, c, nxt=batch_units(n + 1, False)[0]))
            batch(BATCHES - 1, Span(B_FINAL, BATCH), nxt=LAST_OUT)
            c = Span(B_TAIL, TAIL)
            probs_out(c)
            attended(c)
            add_out(c, 0, 0)
            dve.wait_ge(sq_done, 3 * NB)
            inverse_root(c, 0, DM)
            dve.wait_ge(fn_in, 16)
            for b in range(NB):
                nc.vector.scalar_tensor_tensor(out=x1[:, b, :], in0=x1[:, b, :], scalar=rstd[:, b:b + 1], in1=fnorm,
                                               op0=ALU.mult, op1=ALU.mult).then_inc(y_done, 1)

        @block.tensor
        def _(pe):
            def ring(c, plan, name, t, banks, fa, fd, fan, fdn):
                p = t - 4
                while p >= 0 and plan[p] is None:
                    p -= 4
                for who, s, sn in (("A", fa, fan), ("D", fd, fdn)):
                    if p >= 0:
                        if plan[p] == who:
                            pe.wait_ge(s, c(sn, plan[:p + 1].count(who)))
                    else:
                        w = c(sn, 0)
                        if not isinstance(w, int) or w:
                            pe.wait_ge(s, w)
                return banks[c.parity(name, t, 4)]

            def pj(c, plan, t):
                return ring(c, plan, "pj_slots", t, PJ, pj_fa, pj_fd, "pj_fa", "pj_fd")

            def att(c, plan, t):
                return ring(c, plan, "at_slots", t, AT, at_fa, at_fd, "at_fa", "at_fd")

            def product(out_ap, stat_, mov, start, stop):
                for i, (a, b) in enumerate(((0, 0), (0, 1), (1, 0))):
                    ins = nc.tensor.matmul(out_ap, stat_[a], mov[b], start=start and i == 0, stop=stop and i == 2)
                return ins

            def weights(c, k, unit):
                slot = c.parity("unit", k, 2)
                pe.wait_ge(lo_done, c("unit", k + 1))
                return [unit_view(t[slot], unit) for t in (whi, wlo)]

            def features_out(c, plan, k, unit, tile):
                w = weights(c, k, unit)
                for m in range(unit[2] // P):
                    o = pj(c, plan, tile + m)
                    for kk in range(KC):
                        ins = product(o[:, :], [x_[:, kk, m * P:(m + 1) * P] for x_ in w],
                                      [t[:, kk, :] for t in hT], kk == 0, kk == KC - 1)
                    ins.then_inc(pj_full, 1)
                return ins

            def tokens_out(c, plan, k, unit, tile, pick):
                w = weights(c, k, unit)
                for s in range(NB):
                    if s % 2 == 0:
                        o = pj(c, plan, tile + s // 2)
                    for kk in range(KC):
                        ins = product(o[:, (s % 2) * UW:(s % 2 + 1) * UW], [pick(t, kk, s) for t in hT],
                                      [x_[:, kk, :] for x_ in w], kk == 0, kk == KC - 1)
                    if s % 2 == 1:
                        ins.then_inc(pj_full, 1)

            def out_proj(c, plan, k, unit, tile, o_parts, c0):
                w = weights(c, k, unit)
                for t in range(8):
                    s, nh = t // 2, t % 2
                    o = pj(c, plan, tile + t)
                    for cc in range(2):
                        ins = product(o[:, :], [x_[:, c0 + cc, s * P:(s + 1) * P] for x_ in o_parts],
                                      [x_[:, cc, nh * 512:(nh + 1) * 512] for x_ in w], cc == 0, cc == 1)
                    ins.then_inc(pj_full, 1)

            def block_of(t, kk, s):
                return t[:, kk, s * P:(s + 1) * P]

            def class_of(t, kk, s):
                return t[:, kk, s:SEQ:4]

            def rows_transposed(c, plan, done):
                for k in range(KC):
                    o = att(c, plan, k)
                    if k == 0:
                        pe.wait_ge(xn_done, done)
                    for b in range(NB):
                        ins = nc.tensor.transpose(o[:, b * P:(b + 1) * P], big[:, b, k * P:(k + 1) * P], ident)
                    ins.then_inc(at_full, 1)

            c = Span(B_PRO, PRO)
            pe.wait_ge(c_in, 16)
            rows_transposed(c, AT_PRO, NB)
            pe.wait_ge(lr_split, 1)
            pe.wait_ge(at_fd, KC)
            o = att(c, AT_PRO, 8)
            for s in range(NB):
                for kk in range(KC):
                    ins = product(o[:, s * RANK:(s + 1) * RANK], [block_of(t, kk, s) for t in hT],
                                  [t[:, kk, :] for t in lr_w], kk == 0, kk == KC - 1)
            ins.then_inc(at_full, 1)
            features_out(c, PJ_PRO, 0, FIRST_QK[0], 0)
            pe.wait_ge(at_fa, 1)
            o = att(c, AT_PRO, 9)
            for s in range(NB):
                ins = nc.tensor.transpose(o[0:RANK, s * P:(s + 1) * P], lr_n[:, s * RANK:(s + 1) * RANK], ident)
            ins.then_inc(at_full, 1)
            features_out(c, PJ_PRO, 1, FIRST_QK[1], 2)
            pe.wait_ge(at_fd, KC + 1)
            pe.wait_ge(lr_in, 48)
            for b in range(NB):
                o = att(c, AT_PRO, 10 + b)
                nc.tensor.matmul(o[:, :], lrT[0:RANK + 1, b * P:(b + 1) * P], wup[0:RANK + 1, :],
                                 start=True, stop=True).then_inc(at_full, 1)
            pe.wait_ge(at_fd, KC + 5)
            for h in range(GH):
                o = att(c, AT_PRO, 14 + h)
                for b in range(NB):
                    ins = nc.tensor.matmul(o[:, b * P:(b + 1) * P], lgate[:, b, h * P:(h + 1) * P], tri,
                                           start=True, stop=True)
                ins.then_inc(at_full, 1)

            def head(h, c, last=False):
                units = head_units(h, last)
                plan = PJ_LAST if last else PJ_HEAD

                def level(i):
                    o = att(c, AT_HEAD, i)
                    if i < NL:
                        pe.wait_ge(lvq, c("lvq", i + 1))
                    src = qkd[:, i % 2, :, :] if i < NL else qk
                    for b in range(NB):
                        w = slice(b * P, (b + 1) * P)
                        ins = nc.tensor.matmul(o[:, w], src[:, 1, w], src[:, 0, w], start=True, stop=True)
                    ins.then_inc(at_full, 1)

                pe.wait_ge(pj_fa, c("pj_fa", 0))
                tokens_out(c, plan, 0, units[0], 0, block_of)
                for i in range(0, 3):
                    level(i)
                tokens_out(c, plan, 1, units[1], 2, block_of)
                for i in range(3, 6):
                    level(i)
                tokens_out(c, plan, 2, units[2], 4, block_of)
                level(6)
                level(7)
                pe.wait_ge(qd_done, c("qd", 1))
                o = att(c, AT_HEAD, NL + 1)
                nc.tensor.matmul(o[:, 0:128], kd[:, 0, :], qd[:, 0, :], start=True, stop=True)
                nc.tensor.matmul(o[:, 128:384], kd[:, 3, :], qd[:, 1:3, :].rearrange("p a b -> p (a b)"),
                                 start=True, stop=True).then_inc(at_full, 1)
                o = att(c, AT_HEAD, NL + 2)
                nc.tensor.matmul(o[:, 0:256], kd[:, 1, :], qd[:, 1:3, :].rearrange("p a b -> p (a b)"),
                                 start=True, stop=True)
                nc.tensor.matmul(o[:, 256:384], kd[:, 2, :], qd[:, 3, :], start=True, stop=True).then_inc(at_full, 1)
                tokens_out(c, plan, 3, units[3], 6, block_of)
                pe.wait_ge(ats, c("ats", 1))
                pe.wait_ge(at_fd, c("at_fd", NL + 3))
                pe.wait_ge(pj_fd, c("pj_fd", 4))
                between = {(0, 1): 4, (0, 2): 5, (0, 3): 6, (1, 2): 7, (1, 3): 8, (2, 3): 9}
                for i in range(NB):
                    o = att(c, AT_HEAD, NL + 3 + i)
                    for j in range(i + 1):
                        k = i if j == i else between[j, i]
                        ins = product(o[:, :], [t[:, k, :] for t in at], [t[:, j, :] for t in vr], j == 0, j == i)
                    ins.then_inc(at_full, 1)
                k = 4
                if not last:
                    features_out(c, plan, 4, units[4], 8)
                    features_out(c, plan, 5, units[5], 10)
                    k = 6
                pe.wait_ge(at_fd, c("at_fd", NL + 7))
                for i in range(4):
                    o = att(c, AT_HEAD, NL + 7 + i)
                    for b in range(NB):
                        ins = nc.tensor.transpose(o[:, b * P:(b + 1) * P], gate[:, b, i * P:(i + 1) * P], ident)
                    ins.then_inc(at_full, 1)
                pe.wait_ge(at_fd, c("at_fd", NL + 11))
                tile = 8 if last else 12
                out_proj(c, plan, k, units[k], tile, oT, 0)
                out_proj(c, plan, k + 1, units[k + 1], tile + 8, oT, 2)

            turns(pe, 0, GH - 1, B_HEAD, HEAD, head)
            head(GH - 1, Span(B_LAST, LAST), True)
            rows_transposed(Span(B_MID, MID), AT_MID, 2 * NB)
            pe.wait_ge(at_fd, B_FIRST["at_fd"])

            def turned(c, plan):
                blocks = []
                for j in range(2):
                    blocks += [s0[:, j, b * P:(b + 1) * P] for b in range(7)]
                    blocks += [s12[j][:, r, g * P:(g + 1) * P] for r in range(4) for g in range(2)]
                pe.wait_ge(nrm_done, c("nrm", 0))
                for t in range(8):
                    o = att(c, plan, t)
                    for i, p in enumerate(blocks[4 * t:4 * t + 4]):
                        ins = nc.tensor.transpose(o[:, i * P:(i + 1) * P], p, ident)
                    ins.then_inc(at_full, 1)

            def attend(c, plan):
                pe.wait_ge(at_fa, c("at_fa", 4))
                pe.wait_ge(at_fd, c("at_fd", 4))
                for j in range(2):
                    w = slice(j * P, (j + 1) * P)
                    o = att(c, plan, 8 + 2 * j)
                    for b in range(NB):
                        d = o[:, b * P:(b + 1) * P]
                        if b:
                            nc.tensor.matmul(d, vv[0][:, b - 1, w], pT[:, 15 * j + 2 * b - 1, :], start=True, stop=False)
                        ins = nc.tensor.matmul(d, vv[0][:, b, w], pT[:, 15 * j + 2 * b, :], start=b == 0, stop=True)
                    ins.then_inc(at_full, 1)
                    o = att(c, plan, 9 + 2 * j)
                    for r in range(4):
                        d = o[:, r * P:(r + 1) * P]
                        for g in range(2):
                            ins = nc.tensor.matmul(d, vv[1 + g][:, r, w], pT[:, 15 * j + 7 + 2 * r + g, :],
                                                   start=g == 0, stop=g == 1)
                    ins.then_inc(at_full, 1)

            def batch(n, c, first=False):
                units = batch_units(n, first)
                pj_plan, at_plan = (PJ_FIRST, AT_FIRST) if first else (PJ_BATCH, AT_BATCH)
                a0 = 0 if first else 12

                def scores(g):
                    q, k = qT[g % 2], kT[g % 2]
                    pe.wait_ge(pj_fa, c("pj_fa", 4 * g + 4))
                    for j in range(2):
                        if g == 0:
                            for half in range(2):
                                o = att(c, at_plan, a0 + 2 * j + half)
                                for b in (2 * half, 2 * half + 1):
                                    kw = slice(max(b - 1, 0) * P, (b + 1) * P)
                                    at0 = (0, 128, 0, 256)[b]
                                    ins = nc.tensor.matmul(o[:, at0:at0 + kw.stop - kw.start], q[:, j, b * P:(b + 1) * P],
                                                           k[:, j, kw], start=True, stop=True)
                                ins.then_inc(at_full, 1)
                        else:
                            o = att(c, at_plan, a0 + 2 + 2 * g + j)
                            for r in range(4):
                                w = slice(r * P, (r + 1) * P)
                                ins = nc.tensor.matmul(o[:, w], q[:, j, w], k[:, j, w], start=True, stop=True)
                            ins.then_inc(at_full, 1)

                features_out(c, pj_plan, 0, units[0], 0)
                if not first:
                    turned(c, at_plan)
                features_out(c, pj_plan, 1, units[1], 2)
                if not first:
                    attend(c, at_plan)
                features_out(c, pj_plan, 2, units[2], 4)
                scores(0)
                features_out(c, pj_plan, 3, units[3], 6)
                features_out(c, pj_plan, 4, units[4], 8)
                scores(1)
                features_out(c, pj_plan, 5, units[5], 10)
                tokens_out(c, pj_plan, 6, units[6], 12, block_of)
                scores(2)
                tokens_out(c, pj_plan, 7, units[7], 14, class_of)
                tokens_out(c, pj_plan, 8, units[8], 16, class_of)
                features_out(c, pj_plan, 9, units[9], 18)
                features_out(c, pj_plan, 10, units[10], 19)
                if not first:
                    pe.wait_ge(ot2, c("ot2", 2))
                    out_proj(c, pj_plan, 11, units[11], 20, oT2, 0)

            batch(0, Span(B_FIRST, FIRST), True)
            turns(pe, 1, BATCHES - 1, B_BATCH, BATCH, batch)
            batch(BATCHES - 1, Span(B_FINAL, BATCH))
            c = Span(B_TAIL, TAIL)
            turned(c, AT_BATCH)
            attend(c, AT_BATCH)
            pe.wait_ge(ot2, c("ot2", 2))
            out_proj(c, ["D"] * 8, 0, LAST_OUT, 0, oT2, 0)


def constants():
    import numpy as np
    t = np.zeros((P, C_END), np.float32)
    i = np.arange(P)
    t[:, C_ID:C_ID + P] = np.eye(P)
    t[:, C_TRI:C_TRI + P] = np.where(i[:, None] <= i[None, :], 1 / 16.0, 0.0)
    tok = 4 * (i % 32) + i // 32
    own = tok[:, None] - i[None, :]
    cls = i[:, None] - i[None, :]
    far = 1e30
    step = 2.0 ** (-8.0 / GROUPS)
    t[:, C_DIST:C_DIST + 128] = np.where(own <= 0, own + 128.0, far)
    t[:, C_DIST + 128:C_DIST + 256] = np.where(own >= 0, own * 1.0, far)
    t[:, C_DIST + 256:C_DIST + 384] = np.where(cls >= 0, cls * 4.0 * step, far)
    t[:, C_DIST + 384:C_DIST + 512] = np.where((cls >= 0) & (cls % 4 == 0), cls * 4.0 * step ** 2, far)
    s, u = i[:, None], i[None, :]
    for k, L in enumerate(LEVELS):
        pair = (s // (2 * L) == u // (2 * L)) & (s % (2 * L) < L) & (u % (2 * L) >= L)
        t[:, C_MASK + k * P:C_MASK + (k + 1) * P] = pair
    t[:, C_MASK + NL * P:C_MASK + (NL + 1) * P] = np.eye(P)
    h = np.arange(HEADS)
    t[:, C_SLOPE:C_SLOPE + HEADS] = -(2.0 ** (-8.0 * (h + 1) / (GROUPS * HEADS))) / QK_SCALE
    return t


def kernel(x, a_norm, a_w_in, a_w_gate_up, a_b_gate, a_g_out, a_w_out, kv_norm, w_kv, b_norm, b_w_in, b_w_out,
           final_norm):
    import numpy as np
    import concourse.bacc as bacc
    from concourse.bass_utils import run_bass_kernel_spmd

    a = {n: np.ascontiguousarray(v) for n, v in dict(
        x=x[0], a_w_in=a_w_in[0], w_gate_up=np.concatenate([a_w_gate_up[0], a_b_gate[0:1]], 0), a_w_out=a_w_out[0],
        w_kv=w_kv, b_w_in=b_w_in[0], b_w_out=b_w_out[0],
        gains=np.concatenate([np.asarray(g).reshape(-1, P).T for g in (a_norm[0], kv_norm, b_norm[0], a_g_out[0])], 1),
        final_norm=final_norm, consts=constants()).items()}
    nc = bacc.Bacc("TRN2", target_bir_lowering=False, num_devices=1, dynamic_dma_scratch_size=1024)
    aps = [nc.dram_tensor(f"in_{n}", v.shape, mybir.dt.from_np(v.dtype), kind="ExternalInput").ap() for n, v in a.items()]
    o = nc.dram_tensor("out_y", (SEQ, DM), FP, kind="ExternalOutput").ap()
    trunk(nc, *aps, o)
    r = run_bass_kernel_spmd(nc, [{f"in_{n}": v for n, v in a.items()}], core_ids=[0])
    return r.results[0]["out_y"].reshape(1, SEQ, DM)
```

```python
import concourse.bass as bass
from concourse import mybir
from contextlib import ExitStack

FP = mybir.dt.float32
FR = mybir.dt.float32r
I32 = mybir.dt.int32
ALU = mybir.AluOpType
ACT = mybir.ActivationFunctionType
AX = mybir.AxisListType

P = 128
SEQ, DM, DI = 512, 1024, 2048
NB = SEQ // P
KC = DM // P
EPS = 1e-6
GH, DV, RANK = 4, 512, 16
QK_SCALE = 128.0 ** -0.5
VCOL, ZCOL, LRCOL = DM, DM + DI, DM + 2 * DI
HEADS, GROUPS = 16, 3
UW = 256
UE = KC * UW
LEVELS = (64, 32, 16, 8, 4, 2, 1)
NL = len(LEVELS)
BATCHES = HEADS // 2
C_ID, C_TRI, C_DIST, C_MASK = 0, 128, 256, 768
C_SLOPE = C_MASK + 8 * 128
C_END = C_SLOPE + HEADS
G_A, G_KV, G_B, G_OUT = 0, 8, 16, 24

PJ_PRO, AT_PRO = ["A", None] * 2, ["D"] * 13 + ["A"] * 4
PJ_HEAD, AT_HEAD = ["D"] * 8 + ["A", None] * 2 + ["D"] * 16 + [None] * 0, ["D"] * 18 + [None] * 2
PJ_LAST = ["D"] * 24
AT_MID = ["D"] * 8
PJ_FIRST, AT_FIRST = ["A"] * 18 + ["D"] * 2, ["D"] * 8
PJ_BATCH, AT_BATCH = ["A"] * 6 + ["D"] * 8 + ["A"] * 12 + ["D"] * 2, ["A", "D"] * 6 + ["D"] * 8
RSQ = 12


ALL_D, BY_BATCH = ["D"] * 4, ["A", "A", "D", "D"]


def adds(pj, at, tiles_of_units, **more):
    ends = [sum(tiles_of_units[:k + 1]) for k in range(len(tiles_of_units))]
    return dict(more, ends=ends, unit=len(ends), halves=2 * len(ends), pj_slots=len(pj), at_slots=len(at),
                pj_full=len(pj) - pj.count(None), pj_fa=pj.count("A"), pj_fd=pj.count("D"),
                at_full=len(at) - at.count(None), at_fa=at.count("A"), at_fd=at.count("D"))


PER_HEAD = dict(dv=RSQ + 3, lvd=NL, lve=NL + 1, lvq=NL, bh=1, at_hi=2, ats=1, qd=1, sq=4, vh=4, th=4, oth=4)
PER_BATCH = dict(dv=9, zt=2, nb=1, ex=1, nrm=1)
PRO = adds(PJ_PRO, AT_PRO, [1, 1], dv=RSQ)
HEAD = adds(PJ_HEAD, AT_HEAD, [2, 2, 2, 2, 1, 1, 8, 8], **PER_HEAD)
LAST = adds(PJ_LAST, AT_HEAD, [2, 2, 2, 2, 8, 8], **PER_HEAD)
MID = adds([], AT_MID, [], dv=RSQ)
FIRST = adds(PJ_FIRST, AT_FIRST, [2] * 9 + [1, 1], **PER_BATCH)
BATCH = adds(PJ_BATCH, AT_BATCH, [2] * 3 + [8] + [2] * 6 + [1, 1], og2=2, ob=2, ot2=2, **PER_BATCH)
TAIL = adds(["D"] * 8, AT_BATCH[:12], [8], dv=RSQ)


class Span:

    def __init__(self, before, per, turn=None):
        self.before, self.per, self.turn = before, per, turn

    def __call__(self, name, k):
        v = self.before.get(name, 0) + k
        return v if self.turn is None else self.turn * self.per.get(name, 0) + v

    def loads(self, k):
        v = 16 * ((self.before.get("unit", 0) + k) // 2 + 1)
        return v if self.turn is None else self.turn * (8 * self.per["unit"]) + v

    def parity(self, name, k, ring):
        assert self.turn is None or self.per.get(name, 0) % ring == 0
        return (self.before.get(name, 0) + k) % ring


def after(before, per, turns=1):
    names = (set(before) | set(per)) - {"ends"}
    return {k: before.get(k, 0) + turns * per.get(k, 0) for k in names}


B_PRO = {"pj_fd": 4}
B_HEAD = after(B_PRO, PRO)
B_LAST = after(B_HEAD, HEAD, GH - 1)
B_MID = after(B_LAST, LAST)
B_FIRST = after(B_MID, MID)
B_BATCH = after(B_FIRST, FIRST)
B_FINAL = after(B_BATCH, BATCH, BATCHES - 2)
B_TAIL = after(B_FINAL, BATCH)


def trunk(nc, x, a_w_in, w_gate_up, a_w_out, w_kv, b_w_in, b_w_out, gains, final_norm, consts, out):
    ctx = ExitStack()
    with ctx:
        def sb(name, shape, dt=FP):
            return ctx.enter_context(nc.sbuf_tensor(name, shape, dt))

        def sem(name):
            return ctx.enter_context(nc.semaphore(name))

        cst = sb("cst", [P, C_END])
        gain = sb("gain", [P, 28])
        x1 = sb("x1", [P, NB, DM])
        big = sb("big", [P, NB, DM])
        hT = [sb(f"hT_{s}", [P, KC, SEQ], FR) for s in ("hi", "lo")]
        raw = [sb(f"raw{i}", [P, UE]) for i in range(2)]
        whi = [sb(f"whi{i}", [P, UE], FR) for i in range(2)]
        wlo = [sb(f"wlo{i}", [P, UE], FR) for i in range(2)]
        small = sb("small", [P, 96])
        ss, var, rstd, nwt = (small[:, 4 * i:4 * i + 4] for i in range(4))
        scr = sb("scr", [P, 2, 512])
        arena = sb("arena", [P, 13824])
        arena_r = sb("arena_r", [P, 11008], FR)

        def cut(t, at, *shape):
            n = 1
            for d in shape:
                n *= d
            v = t[:, at:at + n]
            if len(shape) == 2:
                v = v.rearrange("p (a b) -> p a b", a=shape[0])
            if len(shape) == 3:
                v = v.rearrange("p (a b c) -> p a b c", a=shape[0], b=shape[1])
            return v

        ident = cst[:, C_ID:C_ID + P]
        tri = cst[:, C_TRI:C_TRI + P]
        bT = cut(arena, 0, GH, SEQ)
        qk = cut(arena, 2048, 2, SEQ)
        ee = cut(arena, 3072, 2, SEQ)
        qkd = cut(arena, 4096, 2, 2, SEQ)
        atd = cut(arena, 6144, NB, P)
        e1 = cut(arena, 6656, 3, P)
        e2 = cut(arena, 7040, 3, P)
        qd = cut(arena, 7424, 4, P)
        kd = cut(arena, 7936, 4, P)
        gate = big[:, 0:2, :].rearrange("p a (b c) -> p (a b) c", b=2)
        lgate = big[:, 2:4, :].rearrange("p a (b c) -> p (a b) c", b=2)
        lrT = arena[:, 8512:9024]
        wup = arena[:, 9024:9536]
        raw_lr = cut(arena, 9536, KC, RANK)
        etot = arena[:, 9664:9668]
        bh = arena[:, 9668:10180]
        tick = arena[:, 10180:10181]
        at = [cut(arena_r, 0, 10, P), cut(arena_r, 1280, 10, P)]
        lr_w = [cut(arena_r, 2560, KC, RANK), cut(arena_r, 2688, KC, RANK)]
        vr = [cut(arena_r, 6912, NB, DV), cut(arena_r, 8960, NB, DV)]
        oT = [cut(arena_r, 2816, NB, SEQ), cut(arena_r, 4864, NB, SEQ)]
        qT = [cut(arena, 1024 * i, 2, SEQ) for i in range(2)]
        kT = [cut(arena, 2048, 2, SEQ), big[:, 3, :].rearrange("p (j t) -> p j t", j=2)]
        vv = [cut(arena, 3072 + 1024 * g, NB, UW) for g in range(GROUPS)]
        s0 = cut(arena, 6144, 2, 896)
        s12 = [cut(arena, 7936 + 1024 * j, NB, 256) for j in range(2)]
        pT = cut(arena, 9984, 30, P)
        gate2 = big[:, 2, :].rearrange("p (j t) -> p j t", j=2)
        o_sum = big[:, 0, :].rearrange("p (j t) -> p j t", j=2)
        oT2 = [cut(arena_r, 0, 2, SEQ), cut(arena_r, 1024, 2, SEQ)]
        fnorm = big[:, 1, :]
        xg = cut(arena, 0, NB, DM)

        def stat(k):
            return small[:, 16 + 16 * k:32 + 16 * k].rearrange("p (l j b) -> p l j b", l=2, j=2)

        mx, nbias, lsum, rinv, xch = (stat(k) for k in range(5))
        PJ = [ctx.enter_context(nc.psum_tensor(f"PJ{i}", [P, 512], FP)) for i in range(4)]
        AT = [ctx.enter_context(nc.psum_tensor(f"AT{i}", [P, 512], FP)) for i in range(4)]

        raw_full = [sem("raw_full0"), sem("raw_full1")]
        hi_done, lo_done = sem("hi_done"), sem("lo_done")
        pj_full, pj_fa, pj_fd = sem("pj_full"), sem("pj_fa"), sem("pj_fd")
        at_full, at_fa, at_fd = sem("at_full"), sem("at_fa"), sem("at_fd")
        dv = sem("dv")
        x_in = [sem(f"x_in{b}") for b in range(NB)]
        c_in, m_in, lr_in, fn_in = (sem(n) for n in ("c_in", "m_in", "lr_in", "fn_in"))
        sq_done, xn_done, ht_hi = sem("sq_done"), sem("xn_done"), sem("ht_hi")
        lr_hi, lr_split, ones_set = sem("lr_hi"), sem("lr_split"), sem("ones_set")
        u_abs, u_exp, u_ln = sem("u_abs"), sem("u_exp"), sem("u_ln")
        y_done, xg_done, out_done = [sem(f"y_done{b}") for b in range(NB)], sem("xg_done"), sem("out_done")
        bh_done, lvd, lve, lvq, at_hi, ats = (sem(n) for n in ("bh_done", "lvd", "lve", "lvq", "at_hi", "ats"))
        qd_done, head_sq, vh, th, oth = (sem(n) for n in ("qd_done", "head_sq", "vh", "th", "oth"))
        nb_done, ex_done, nrm_done, zt = (sem(n) for n in ("nb_done", "ex_done", "nrm_done", "zt"))
        og2, ob, ot2 = (sem(n) for n in ("og2", "ob", "ot2"))

        def by_rows(w):
            return w.rearrange("(k p) c -> p k c", p=P)

        w_a, w_b, w_s = by_rows(a_w_in), by_rows(b_w_in), by_rows(w_kv)
        o_a, o_b = by_rows(a_w_out), by_rows(b_w_out)

        def in_unit(w, col, cols, g):
            return (w[:, :, bass.ds(col, cols)], KC, cols, g)

        def out_unit(w, row, g):
            return (w[:, bass.ds(row, 2), :], 2, DM, g)

        def v_a(h, u):
            return in_unit(w_a, h * DV + (VCOL + u * UW), UW, G_A)

        def z_a(h, u):
            return in_unit(w_a, h * DV + (ZCOL + u * UW), UW, G_A)

        def qk_a(h, i):
            return in_unit(w_a, h * P + i * GH * P, P, G_A)

        def head_units(h, last):
            mid = [] if last else [qk_a(h + 1, 0), qk_a(h + 1, 1)]
            return ([v_a(h, 0), v_a(h, 1), z_a(h, 0), z_a(h, 1)] + mid
                    + [out_unit(o_a, h * 4 + 2 * u, G_OUT + 2 * u) for u in range(2)])

        def batch_units(n, first):
            u = []
            for g in range(GROUPS):
                u += [in_unit(w_b, n * UW + g * DI, UW, G_B), in_unit(w_s, n * UW + g * DI, UW, G_KV)]
            u += [in_unit(w_s, n * UW + (GROUPS + g) * DI, UW, G_KV) for g in range(GROUPS)]
            u += [in_unit(w_b, n * UW + (GROUPS * DI + j * P), P, G_B) for j in range(2)]
            return u if first else u[:3] + [out_unit(o_b, n * 2 + (-2), None)] + u[3:]

        FIRST_QK = [qk_a(0, 0), qk_a(0, 1)]
        LAST_OUT = out_unit(o_b, HEADS - 2, None)

        def unit_view(t, unit):
            _, k, cols, _ = unit
            return t[:, 0:k * cols].rearrange("p (k c) -> p k c", k=k)

        def turns(eng, lo, hi, before, per, body):
            with eng.Fori(0, hi - lo) as i:
                body(i + lo, Span(before, per, i))

        block = ctx.enter_context(nc.Block())

        @block.sync
        def _(sp):
            def load(c, k, unit):
                u = c("unit", k)
                slot = c.parity("unit", k, 2)
                if not isinstance(u, int) or u >= 2:
                    sp.wait_ge(lo_done, c("halves", 2 * k - 2))
                sp.dma_start(unit_view(raw[slot], unit), unit[0]).then_inc(raw_full[slot], 16)

            for b in range(NB):
                sp.dma_start(x1[:, b, :], x[b * P:(b + 1) * P, :]).then_inc(x_in[b], 16)
            c = Span(B_PRO, PRO)
            for k, unit in enumerate(FIRST_QK):
                load(c, k, unit)

            def head(h, c, last=False):
                for k, unit in enumerate(head_units(h, last)):
                    load(c, k, unit)

            turns(sp, 0, GH - 1, B_HEAD, HEAD, head)
            head(GH - 1, Span(B_LAST, LAST), True)

            def batch(n, c, first=False):
                for k, unit in enumerate(batch_units(n, first)):
                    load(c, k, unit)

            batch(0, Span(B_FIRST, FIRST), True)
            turns(sp, 1, BATCHES - 1, B_BATCH, BATCH, batch)
            batch(BATCHES - 1, Span(B_FINAL, BATCH))
            load(Span(B_TAIL, TAIL), 0, LAST_OUT)
            sp.wait_ge(at_fd, B_FIRST["at_fd"])
            sp.dma_start(fnorm, final_norm.rearrange("(a n) -> a n", a=1).to_broadcast([P, DM])).then_inc(fn_in, 16)
            for b in range(NB):
                sp.wait_ge(y_done[b], 1)
                sp.dma_start(out[b * P:(b + 1) * P, :], xg[:, b, :]).then_inc(out_done, 16)
            sp.wait_ge(out_done, 64)

        @block.gpsimd
        def _(pool):
            pool.memset(lrT[0:32, :], 1.0).then_inc(ones_set, 1)

            def head(h, c):
                pool.wait_ge(bh_done, c("bh", 1))
                for i, L in enumerate(LEVELS):
                    v = bh[:, :].rearrange("p (n u l) -> p n u l", u=2, l=L)
                    d = ee[:, i % 2, :].rearrange("p (n u l) -> p n u l", u=2, l=L)
                    ref = v[:, :, 0, L - 1:L].to_broadcast([P, SEQ // (2 * L), L])
                    w = c("lvq", max(i - 1, 0))
                    if not isinstance(w, int) or w:
                        pool.wait_ge(lvq, w)
                    pool.tensor_tensor(d[:, :, 0, :], ref, v[:, :, 0, :], ALU.subtract)
                    pool.tensor_tensor(d[:, :, 1, :], v[:, :, 1, :], ref, ALU.subtract).then_inc(lvd, 1)

            turns(pool, 0, GH - 1, B_HEAD, HEAD, head)
            head(GH - 1, Span(B_LAST, LAST))

        @block.scalar
        def _(act):
            def hi(c, k, unit):
                slot = c.parity("unit", k, 2)
                u = c("unit", k)
                act.wait_ge(raw_full[slot], c.loads(k))
                if not isinstance(u, int) or u >= 2:
                    act.wait_ge(pj_full, c("pj_full", c.per["ends"][k - 2] if k >= 2 else 0))
                src, dst = unit_view(raw[slot], unit), unit_view(whi[slot], unit)
                half = unit[1] // 2
                for m in range(2):
                    if unit[3] is None:
                        nc.scalar.activation(dst[:, m, :], src[:, m, :], ACT.Copy).then_inc(hi_done, 1)
                        continue
                    for j in range(m * half, (m + 1) * half):
                        ins = nc.scalar.activation(dst[:, j, :], src[:, j, :], ACT.Copy,
                                                   scale=gain[:, unit[3] + j:unit[3] + j + 1])
                    ins.then_inc(hi_done, 1)

            def squares(src, done, added=None):
                for b in range(NB):
                    if added is None:
                        act.wait_ge(x_in[b], 16)
                    else:
                        act.wait_ge(pj_fd, added - 6 + 2 * b)
                    if b:
                        act.wait_ge(sq_done, done + b)
                    nc.scalar.activation(scr[:, :, :].rearrange("p a b -> p (a b)"), src[:, b, :], ACT.Square,
                                         accum_out=ss[:, b:b + 1]).then_inc(sq_done, 1)

            def transposed(c, done):
                for k in range(KC):
                    act.wait_ge(at_full, c("at_full", k + 1))
                    nc.scalar.activation(hT[0][:, k, :], AT[c.parity("at_slots", k, 4)][:, :],
                                         ACT.Copy).then_inc(ht_hi, 1)

            def normalised(c):
                act.wait_ge(dv, c("dv", RSQ))
                for b in (1, 3):
                    nc.scalar.activation(big[:, b, :], x1[:, b, :], ACT.Copy, scale=rstd[:, b:b + 1]).then_inc(xn_done, 1)

            act.dma_start(cst[:, 0:C_DIST], consts[:, 0:C_DIST]).then_inc(c_in, 16)
            act.dma_start(gain[:, :], gains).then_inc(lr_in, 16)
            act.dma_start(raw_lr[:, :, :], w_a[:, :, LRCOL:LRCOL + RANK]).then_inc(lr_in, 16)
            act.dma_start(wup[0:RANK + 1, :], w_gate_up).then_inc(lr_in, 16)
            act.dma_start(cst[:, C_DIST:C_END], consts[:, C_DIST:C_END]).then_inc(m_in, 16)
            c = Span(B_PRO, PRO)
            squares(x1, 0)
            act.wait_ge(lr_in, 48)
            for j in range(KC):
                ins = nc.scalar.activation(lr_w[0][:, j, :], raw_lr[:, j, :], ACT.Copy, scale=gain[:, j:j + 1])
            ins.then_inc(lr_hi, 1)
            hi(c, 0, FIRST_QK[0])
            normalised(c)
            transposed(c, 0)
            hi(c, 1, FIRST_QK[1])
            hi(c, 2, v_a(0, 0))
            for b in range(NB):
                act.wait_ge(at_full, KC + 2 + b)
                nc.scalar.activation(scr[:, b % 2, :], AT[(KC + 1 + b) % 4][:, :], ACT.Abs).then_inc(u_abs, 1)
                act.wait_ge(u_abs, b + 1)
                nc.scalar.activation(gate[:, b, :], scr[:, b % 2, :], ACT.Exp, scale=-1.0).then_inc(u_exp, 1)
            for b in range(NB):
                act.wait_ge(u_exp, b + 1)
                nc.scalar.activation(lgate[:, b, :], gate[:, b, :], ACT.Ln, bias=1.0).then_inc(u_ln, 1)
            for h in range(GH):
                act.wait_ge(at_full, KC + 6 + h)
                nc.scalar.activation(bT[:, h, :], AT[(KC + 5 + h) % 4][:, :], ACT.Copy).then_inc(at_fa, 1)

            def q_or_k(c, i, tile, pj_index):
                act.wait_ge(pj_full, c("pj_full", pj_index + 1))
                nc.scalar.activation(qk[:, i, :], PJ[tile % 4][:, :], ACT.Copy,
                                     scale=QK_SCALE if i == 0 else 1.0).then_inc(pj_fa, 1)

            for i in range(2):
                q_or_k(c, i, 2 * i, i)

            def head(h, c, last=False, nxt=None):
                units = head_units(h, last) + [nxt(h)]
                b = bh[:, :].rearrange("p (n t) -> p n t", t=P)

                def value_hi(u):
                    for i in range(2):
                        t = 2 * u + i
                        act.wait_ge(pj_full, c("pj_full", t + 1))
                        nc.scalar.activation(vr[0][:, 2 * i:2 * i + 2, u * UW:(u + 1) * UW],
                                             PJ[t % 4][:, :].rearrange("p (s c) -> p s c", s=2),
                                             ACT.Copy).then_inc(vh, 1)

                def tanh(u):
                    for i in range(2):
                        t = 4 + 2 * u + i
                        act.wait_ge(pj_full, c("pj_full", t + 1))
                        act.wait_ge(pj_fd, c("pj_fd", t - 2))
                        nc.scalar.activation(scr[:, i, :], PJ[t % 4][:, :], ACT.Tanh, scale=0.5).then_inc(th, 1)

                def exps(lo, up):
                    for i in range(lo, up):
                        act.wait_ge(lvd, c("lvd", i + 1))
                        nc.scalar.activation(ee[:, i % 2, :], ee[:, i % 2, :], ACT.Exp).then_inc(lve, 1)

                act.wait_ge(at_fa, c("at_fa", 0))
                w = c("lvq", 0)
                if not isinstance(w, int) or w:
                    act.wait_ge(lvd, c("lvd", 0))
                nc.scalar.activation(bh[:, :].unsqueeze(1), bT[:, bass.ds(h, 1), :], ACT.Copy).then_inc(bh_done, 1)
                hi(c, 1, units[1])
                exps(0, 4)
                value_hi(0)
                hi(c, 2, units[2])
                exps(4, 6)
                nc.scalar.activation(e1[:, :, :], b[:, 1:4, :], ACT.Exp)
                nc.scalar.activation(etot, b[:, :, P - 1], ACT.Exp)
                for s in range(3):
                    ins = nc.scalar.activation(e2[:, s, :], b[:, s, :], ACT.Exp, scale=-1.0, bias=b[:, s, P - 1:P])
                ins.then_inc(lve, 1)
                exps(NL - 1, NL)
                value_hi(1)
                hi(c, 3, units[3])
                tanh(0)
                act.wait_ge(at_fd, c("at_fd", NL + 1))
                nc.scalar.activation(at[0][:, 0:4, :], atd[:, :, :], ACT.Copy).then_inc(at_hi, 1)
                for i in range(2):
                    act.wait_ge(at_full, c("at_full", NL + 2 + i))
                    ins = nc.scalar.activation(at[0][:, 4 + 3 * i:7 + 3 * i, :].rearrange("p a b -> p (a b)"),
                                               AT[c.parity("at_slots", NL + 1 + i, 4)][:, 0:384], ACT.Copy)
                ins.then_inc(at_hi, 1)
                hi(c, 4, units[4])
                tanh(1)
                hi(c, 5, units[5])
                act.wait_ge(pj_fd, c("pj_fd", 8))
                for i in range(NB):
                    act.wait_ge(at_full, c("at_full", NL + 4 + i))
                    if i >= 2:
                        act.wait_ge(head_sq, c("sq", i - 1))
                    nc.scalar.activation(scr[:, i % 2, :], AT[c.parity("at_slots", NL + 3 + i, 4)][:, :],
                                         ACT.Square, accum_out=ss[:, i:i + 1]).then_inc(head_sq, 1)
                if not last:
                    act.wait_ge(qd_done, c("qd", 1))
                    q_or_k(c, 0, 8, 8)
                    hi(c, 6, units[6])
                    q_or_k(c, 1, 10, 9)
                for i in range(4):
                    act.wait_ge(at_full, c("at_full", NL + 8 + i))
                    nc.scalar.activation(oT[0][:, i, :], AT[c.parity("at_slots", NL + 7 + i, 4)][:, :],
                                         ACT.Copy).then_inc(oth, 1)
                for k in range(6 if last else 7, len(units)):
                    hi(c, k, units[k])

            turns(act, 0, GH - 1, B_HEAD, HEAD, lambda h, c: head(h, c, nxt=lambda h: v_a(h + 1, 0)))
            head(GH - 1, Span(B_LAST, LAST), True, nxt=lambda h: batch_units(0, True)[0])

            c = Span(B_MID, MID)
            squares(x1, NB, c("pj_fd", 0))
            normalised(c)
            transposed(c, KC)

            def batch(n, c, first=False, nxt=None):
                units = batch_units(n, first) + [nxt]

                def copy(tile, dst, src=None):
                    act.wait_ge(pj_full, c("pj_full", tile + 1))
                    bank = PJ[tile % 4][:, :]
                    nc.scalar.activation(dst, bank if src is None else src(bank), ACT.Copy).then_inc(pj_fa, 1)

                def heads(tile, dst, order):
                    for j in range(2):
                        if order == "tokens":
                            copy(tile + j, dst[:, j, :])
                        elif order == "blocks":
                            copy(tile + j, dst[:, j, :].rearrange("p (b r i) -> p b r i", b=NB, r=4),
                                 lambda t: t.rearrange("p (b i r) -> p b r i", b=NB, r=4))
                        else:
                            copy(tile + j, dst[:, j, :].rearrange("p (r j) -> p r j", r=4),
                                 lambda t: t.rearrange("p (j r) -> p r j", r=4))

                def value(g, tile, i):
                    copy(tile + i, vv[g][:, 2 * i:2 * i + 2, :], lambda t: t.rearrange("p (s c) -> p s c", s=2))

                def values(g, tile):
                    value(g, tile, 0)
                    value(g, tile, 1)

                hi(c, 1, units[1])
                if not first:
                    for t in range(0, 8, 2):
                        act.wait_ge(at_full, c("at_full", t + 1))
                        nc.scalar.activation(pT[:, 4 * t:4 * t + 4, :].rearrange("p a b -> p (a b)"),
                                             AT[c.parity("at_slots", t, 4)][:, :], ACT.Copy).then_inc(at_fa, 1)
                heads(0, qT[0], "blocks")
                hi(c, 2, units[2])
                heads(2, kT[0], "tokens")
                if not first:
                    attended_act(c)
                hi(c, 3, units[3])
                heads(4, qT[1], "classes")
                k, t = 3, 6
                if not first:
                    hi(c, 4, units[4])
                    k, t = 4, 14
                hi(c, k + 1, units[k + 1])
                heads(t, kT[1], "classes")
                hi(c, k + 2, units[k + 2])
                heads(t + 2, qT[0], "classes")
                hi(c, k + 3, units[k + 3])
                heads(t + 4, kT[0], "classes")
                hi(c, k + 4, units[k + 4])
                values(0, t + 6)
                hi(c, k + 5, units[k + 5])
                values(1, t + 8)
                hi(c, k + 6, units[k + 6])
                act.wait_ge(nb_done, c("nb", 1))
                for j in range(2):
                    for b in range(NB):
                        w = slice(max(256 * b - 128, 0), 256 * b + 128)
                        nc.scalar.activation(s0[:, j, w], s0[:, j, w], ACT.Exp, scale=QK_SCALE,
                                             bias=nbias[:, 0, j, b:b + 1], accum_out=lsum[:, 0, j, b:b + 1])
                        ins = nc.scalar.activation(s12[j][:, b, :], s12[j][:, b, :], ACT.Exp, scale=QK_SCALE,
                                                   bias=nbias[:, 1, j, b:b + 1], accum_out=lsum[:, 1, j, b:b + 1])
                    if j == 0:
                        value(2, t + 10, 0)
                ins.then_inc(ex_done, 1)
                value(2, t + 10, 1)
                for j in range(2):
                    hi(c, k + 7 + j, units[k + 7 + j])
                    act.wait_ge(pj_full, c("pj_full", t + 13 + j))
                    nc.scalar.activation(scr[:, j, :], PJ[(t + 12 + j) % 4][:, :], ACT.Tanh, scale=0.5).then_inc(zt, 1)

            def attended_act(c):
                for j in range(2):
                    act.wait_ge(at_full, c("at_full", 9 + 2 * j))
                    nc.scalar.activation(o_sum[:, j, :].rearrange("p (b i r) -> p b r i", b=NB, r=4),
                                         AT[c.parity("at_slots", 8 + 2 * j, 4)][:, :].rearrange(
                                             "p (b r i) -> p b r i", b=NB, r=4), ACT.Copy).then_inc(at_fa, 1)
                for j in range(2):
                    act.wait_ge(og2, c("og2", j + 1))
                    nc.scalar.activation(oT2[0][:, j, :], o_sum[:, j, :], ACT.Copy).then_inc(ob, 1)

            batch(0, Span(B_FIRST, FIRST), True, batch_units(1, False)[0])
            turns(act, 1, BATCHES - 1, B_BATCH, BATCH,
                  lambda n, c: batch(n, c, nxt=batch_units(n + 1, False)[0]))
            batch(BATCHES - 1, Span(B_FINAL, BATCH), nxt=LAST_OUT)
            c = Span(B_TAIL, TAIL)
            for t in range(0, 8, 2):
                act.wait_ge(at_full, c("at_full", t + 1))
                nc.scalar.activation(pT[:, 4 * t:4 * t + 4, :].rearrange("p a b -> p (a b)"),
                                     AT[c.parity("at_slots", t, 4)][:, :], ACT.Copy).then_inc(at_fa, 1)
            attended_act(c)
            squares(x1, 2 * NB, c("pj_fd", 8))
            act.wait_ge(dv, c("dv", RSQ))
            for b in (1, 3):
                act.wait_ge(xg_done, b + 1)
                nc.scalar.activation(xg[:, b, :], xg[:, b, :], ACT.Copy, scale=rstd[:, b:b + 1]).then_inc(y_done[b], 1)

        @block.vector
        def _(dve):
            def link(c, k, ins):
                ins.then_inc(dv, 1)
                dve.wait_ge(dv, c("dv", k + 1))

            def lo(c, k, unit, halves=(0, 1)):
                slot = c.parity("unit", k, 2)
                src, h, dst = (unit_view(t[slot], unit) for t in (raw, whi, wlo))
                h = h.bitcast(FP)
                half = unit[1] // 2
                for m in halves:
                    dve.wait_ge(hi_done, c("halves", 2 * k + m + 1))
                    if unit[3] is None:
                        nc.vector.tensor_tensor(dst[:, m, :], src[:, m, :], h[:, m, :], ALU.subtract).then_inc(lo_done, 1)
                        continue
                    for j in range(m * half, (m + 1) * half):
                        ins = nc.vector.scalar_tensor_tensor(out=dst[:, j, :], in0=src[:, j, :],
                                                             scalar=gain[:, unit[3] + j:unit[3] + j + 1],
                                                             in1=h[:, j, :], op0=ALU.mult, op1=ALU.subtract)
                    ins.then_inc(lo_done, 1)

            def inverse_root(c, k, width):
                v = nc.vector
                link(c, k, v.tensor_scalar(var, ss, 1.0 / width, EPS, ALU.mult, ALU.add))
                link(c, k + 1, v.tensor_scalar(rstd.bitcast(I32), var.bitcast(I32), 1, None, ALU.logical_shift_right))
                link(c, k + 2, v.tensor_scalar(rstd.bitcast(I32), rstd.bitcast(I32), -1.0, float(0x5F3759DF),
                                               ALU.mult, ALU.add))
                for i in range(3):
                    link(c, k + 3 + 3 * i, v.tensor_tensor(nwt, rstd, rstd, ALU.mult))
                    link(c, k + 4 + 3 * i, v.scalar_tensor_tensor(out=nwt, in0=nwt, scalar=-0.5, in1=var,
                                                                  op0=ALU.mult, op1=ALU.mult))
                    last = v.scalar_tensor_tensor(out=rstd, in0=nwt, scalar=1.5, in1=rstd, op0=ALU.add, op1=ALU.mult)
                    link(c, k + 5 + 3 * i, last)

            def normalised(c, done):
                dve.wait_ge(sq_done, done)
                inverse_root(c, 0, DM)
                for b in (0, 2):
                    nc.vector.tensor_scalar(big[:, b, :], x1[:, b, :], rstd[:, b:b + 1], None,
                                            ALU.mult).then_inc(xn_done, 1)

            def transposed_lo(c, done):
                for k in range(KC):
                    dve.wait_ge(ht_hi, done + k + 1)
                    nc.vector.tensor_tensor(hT[1][:, k, :], AT[c.parity("at_slots", k, 4)][:, :],
                                            hT[0][:, k, :].bitcast(FP), ALU.subtract).then_inc(at_fd, 1)

            nc.vector.memset(tick, 0.0).then_inc(pj_fd, 4)
            c = Span(B_PRO, PRO)
            normalised(c, NB)
            dve.wait_ge(lr_hi, 1)
            for j in range(KC):
                ins = nc.vector.scalar_tensor_tensor(out=lr_w[1][:, j, :], in0=raw_lr[:, j, :], scalar=gain[:, j:j + 1],
                                                     in1=lr_w[0].bitcast(FP)[:, j, :], op0=ALU.mult, op1=ALU.subtract)
            ins.then_inc(lr_split, 1)
            lo(c, 0, FIRST_QK[0])
            transposed_lo(c, 0)
            lo(c, 1, FIRST_QK[1])
            dve.wait_ge(at_full, KC + 1)
            dve.wait_ge(ones_set, 1)
            nc.vector.tensor_copy(lrT[0:RANK, :], AT[KC % 4][0:RANK, :]).then_inc(at_fd, 1)
            lo(c, 2, v_a(0, 0))
            for b in range(NB):
                dve.wait_ge(u_ln, b + 1)
                nc.vector.scalar_tensor_tensor(out=lgate[:, b, :], in0=AT[(KC + 1 + b) % 4][:, :], scalar=0.0,
                                               in1=lgate[:, b, :], op0=ALU.min, op1=ALU.subtract).then_inc(at_fd, 1)

            def add_out(c, tile, count, first=0, end=8):
                for t in range(first, end):
                    dve.wait_ge(pj_full, c("pj_full", count + t + 1))
                    o = x1[:, t // 2, (t % 2) * 512:(t % 2) * 512 + 512]
                    nc.vector.tensor_tensor(o, PJ[(tile + t) % 4][:, :], o, ALU.add).then_inc(pj_fd, 1)

            def head(h, c, last=False, nxt=None):
                units = head_units(h, last) + [nxt(h)]

                def value_lo(u):
                    for i in range(2):
                        t = 2 * u + i
                        dve.wait_ge(vh, c("vh", t + 1))
                        w = (slice(None), slice(2 * i, 2 * i + 2), slice(u * UW, (u + 1) * UW))
                        nc.vector.tensor_tensor(vr[1][w], PJ[t % 4][:, :].rearrange("p (s c) -> p s c", s=2),
                                                vr[0].bitcast(FP)[w], ALU.subtract).then_inc(pj_fd, 1)

                def gates(u):
                    for i in range(2):
                        t = 4 + 2 * u + i
                        dve.wait_ge(th, c("th", 2 * u + i + 1))
                        nc.vector.scalar_tensor_tensor(
                            out=gate[:, 2 * i:2 * i + 2, u * UW:(u + 1) * UW],
                            in0=scr[:, i, :].rearrange("p (s c) -> p s c", s=2), scalar=1.0,
                            in1=PJ[t % 4][:, :].rearrange("p (s c) -> p s c", s=2),
                            op0=ALU.add, op1=ALU.mult).then_inc(pj_fd, 1)

                def decay(i):
                    dve.wait_ge(lve, c("lve", i + 1 + (i == NL - 1)))
                    w = max(i - 1, 0)
                    dve.wait_ge(at_full, c("at_full", w))
                    nc.vector.tensor_tensor(qkd[:, i % 2, :, :], qk[:, :, :],
                                            ee[:, i % 2, :].unsqueeze(1).to_broadcast([P, 2, SEQ]),
                                            ALU.mult).then_inc(lvq, 1)

                def keep(i):
                    dve.wait_ge(at_full, c("at_full", i + 1))
                    if i == 0:
                        dve.wait_ge(dv, c("dv", 1))
                    else:
                        dve.wait_ge(at_fd, c("at_fd", i))
                    nc.vector.memset(tick, 0.0)
                    m = cst[:, C_MASK + i * P:C_MASK + (i + 1) * P].bitcast(I32)
                    nc.vector.copy_predicated(atd[:, :, :], m.unsqueeze(1).to_broadcast([P, NB, P]),
                                              AT[c.parity("at_slots", i, 4)][:, :].rearrange("p (b t) -> p b t", b=NB))\
                        .then_inc(at_fd, 1)

                lo(c, 1, units[1])
                nc.vector.memset(atd[:, :, :], 0.0).then_inc(dv, 1)
                dve.wait_ge(pj_fa, c("pj_fa", 0))
                decay(0)
                decay(1)
                value_lo(0)
                keep(0)
                decay(2)
                keep(1)
                decay(3)
                lo(c, 2, units[2])
                keep(2)
                decay(4)
                value_lo(1)
                keep(3)
                decay(5)
                lo(c, 3, units[3])
                keep(4)
                decay(6)
                keep(5)
                q4, k4 = (qk[:, i, :].rearrange("p (b t) -> p b t", b=NB) for i in range(2))
                v = nc.vector
                v.tensor_tensor(qd[:, 0:2, :], q4[:, 1:3, :], e1[:, 0:2, :], ALU.mult)
                v.tensor_tensor(qd[:, 3, :], q4[:, 3, :], e1[:, 2, :], ALU.mult)
                link(c, 1, v.tensor_tensor(kd[:, 0:3, :], k4[:, 0:3, :], e2[:, :, :], ALU.mult))
                v.tensor_scalar(qd[:, 2, :], qd[:, 3, :], etot[:, 2:3], None, ALU.mult)
                v.tensor_scalar(kd[:, 3, :], kd[:, 0, :], etot[:, 1:2], None, ALU.mult).then_inc(qd_done, 1)
                gates(0)
                keep(6)
                keep(7)
                dve.wait_ge(at_fd, c("at_fd", NL + 1))
                dve.wait_ge(at_hi, c("at_hi", 1))
                nc.vector.tensor_tensor(at[1][:, 0:4, :], atd[:, :, :], at[0][:, 0:4, :].bitcast(FP),
                                        ALU.subtract).then_inc(ats, 1)
                dve.wait_ge(at_hi, c("at_hi", 2))
                for i in range(2):
                    w = slice(4 + 3 * i, 7 + 3 * i)
                    nc.vector.tensor_tensor(at[1][:, w, :].rearrange("p a b -> p (a b)"),
                                            AT[c.parity("at_slots", NL + 1 + i, 4)][:, 0:384],
                                            at[0][:, w, :].bitcast(FP).rearrange("p a b -> p (a b)"),
                                            ALU.subtract).then_inc(at_fd, 1)
                lo(c, 4, units[4])
                gates(1)
                lo(c, 5, units[5])
                dve.wait_ge(head_sq, c("sq", 4))
                dve.wait_ge(pj_fd, c("pj_fd", 8))
                inverse_root(c, 2, DV)
                link(c, 2 + RSQ, v.tensor_scalar(rstd, rstd, 0.5, None, ALU.mult))
                for i in range(NB):
                    ins = nc.vector.scalar_tensor_tensor(out=gate[:, i, :], in0=AT[c.parity("at_slots", NL + 3 + i, 4)][:, :],
                                                         scalar=rstd[:, i:i + 1], in1=gate[:, i, :],
                                                         op0=ALU.mult, op1=ALU.mult)
                    ins.then_inc(at_fd, 1)
                if not last:
                    lo(c, 6, units[6])
                for i in range(4):
                    dve.wait_ge(oth, c("oth", i + 1))
                    nc.vector.tensor_tensor(oT[1][:, i, :], AT[c.parity("at_slots", NL + 7 + i, 4)][:, :],
                                            oT[0].bitcast(FP)[:, i, :], ALU.subtract).then_inc(at_fd, 1)
                tile, count = (8, 8) if last else (12, 10)
                if last:
                    add_out(c, tile, count)
                    lo(c, 6, units[6])
                    add_out(c, tile + 8, count + 8)
                else:
                    lo(c, 7, units[7])
                    add_out(c, tile, count)
                    add_out(c, tile + 8, count + 8, 0, 2)
                    lo(c, 8, units[8], (0,))
                    add_out(c, tile + 8, count + 8, 2, 4)
                    lo(c, 8, units[8], (1,))
                    add_out(c, tile + 8, count + 8, 4, 8)

            dve.wait_ge(m_in, 16)
            turns(dve, 0, GH - 1, B_HEAD, HEAD, lambda h, c: head(h, c, nxt=lambda h: v_a(h + 1, 0)))
            head(GH - 1, Span(B_LAST, LAST), True, nxt=lambda h: batch_units(0, True)[0])

            c = Span(B_MID, MID)
            normalised(c, 2 * NB)
            transposed_lo(c, KC)

            def swap(c, k, dst, src):
                for a in range(4):
                    for b in range(4):
                        ins = nc.vector.tensor_copy(dst[32 * a:32 * a + 32, :, b], src[32 * b:32 * b + 32, :, a])
                link(c, k, ins)

            def attended(c):
                for j in range(2):
                    dve.wait_ge(at_fa, c("at_fa", 5 + j))
                    dve.wait_ge(at_full, c("at_full", 10 + 2 * j))
                    o = o_sum[:, j, :]
                    by_class = o.rearrange("p (j r) -> p r j", r=4)
                    nc.vector.tensor_tensor(by_class, AT[c.parity("at_slots", 9 + 2 * j, 4)][:, :].rearrange(
                        "p (r j) -> p r j", r=4), by_class, ALU.add).then_inc(at_fd, 1)
                    dve.wait_ge(at_fd, c("at_fd", 5 + j))
                    nc.vector.tensor_tensor(o, o, gate2[:, j, :], ALU.mult).then_inc(og2, 1)
                for j in range(2):
                    dve.wait_ge(ob, c("ob", j + 1))
                    ins = nc.vector.tensor_tensor(oT2[1][:, j, :], o_sum[:, j, :], oT2[0][:, j, :].bitcast(FP),
                                                  ALU.subtract)
                    ins.then_inc(ot2, 1)

            def batch(n, c, first=False, nxt=None):
                units = batch_units(n, first) + [nxt]
                a0 = 0 if first else 12

                def bias0():
                    for j in range(2):
                        sl = slopes(n, j)
                        t0, t1 = (AT[c.parity("at_slots", a0 + 2 * j + i, 4)] for i in range(2))
                        d = cst[:, C_DIST:C_DIST + 256]
                        dve.wait_ge(at_full, c("at_full", a0 + 2 * j + 1))
                        nc.vector.scalar_tensor_tensor(out=s0[:, j, 0:128], in0=d[:, 128:256], scalar=sl,
                                                       in1=t0[:, 0:128], op0=ALU.mult, op1=ALU.add)
                        nc.vector.scalar_tensor_tensor(out=s0[:, j, 128:384], in0=d, scalar=sl,
                                                       in1=t0[:, 128:384], op0=ALU.mult, op1=ALU.add).then_inc(at_fd, 1)
                        dve.wait_ge(at_full, c("at_full", a0 + 2 * j + 2))
                        nc.vector.scalar_tensor_tensor(
                            out=s0[:, j, 384:896].rearrange("p (a k) -> p a k", a=2),
                            in0=d.unsqueeze(1).to_broadcast([P, 2, 256]), scalar=sl,
                            in1=t1[:, :].rearrange("p (a k) -> p a k", a=2), op0=ALU.mult, op1=ALU.add).then_inc(at_fd, 1)

                def bias12(g):
                    for j in range(2):
                        t = a0 + 4 + 2 * (g - 1) + j
                        d = cst[:, C_DIST + 128 + 128 * g:C_DIST + 256 + 128 * g]
                        dve.wait_ge(at_full, c("at_full", t + 1))
                        nc.vector.scalar_tensor_tensor(
                            out=s12[j][:, :, 128 * (g - 1):128 * g], in0=d.unsqueeze(1).to_broadcast([P, 4, 128]),
                            scalar=slopes(n, j), in1=AT[c.parity("at_slots", t, 4)][:, :].rearrange("p (r k) -> p r k", r=4),
                            op0=ALU.mult, op1=ALU.add).then_inc(at_fd, 1)

                lo(c, 1, units[1])
                if not first:
                    probs_out(c)
                lo(c, 2, units[2])
                if not first:
                    attended(c)
                lo(c, 3, units[3])
                bias0()
                k, t = 3, 6
                if not first:
                    lo(c, 4, units[4])
                    add_out(c, 6, 6)
                    k, t = 4, 14
                lo(c, k + 1, units[k + 1])
                lo(c, k + 2, units[k + 2])
                bias12(1)
                lo(c, k + 3, units[k + 3])
                lo(c, k + 4, units[k + 4])
                bias12(2)
                lo(c, k + 5, units[k + 5])
                dve.wait_ge(at_fd, c("at_fd", 8 if first else 14))
                v = nc.vector
                for j in range(2):
                    v.tensor_reduce(mx[:, 0, j, 0:1], s0[:, j, 0:128], AX.X, ALU.max)
                    v.tensor_reduce(mx[:, 0, j, 1:4], s0[:, j, 128:896].rearrange("p (b k) -> p b k", b=3), AX.X, ALU.max)
                    ins = v.tensor_reduce(mx[:, 1, j, :], s12[j][:, :, :], AX.X, ALU.max)
                link(c, 0, ins)
                swap(c, 1, xch[:, 0], mx[:, 1])
                link(c, 2, v.tensor_tensor(mx[:, 0], mx[:, 0], xch[:, 0], ALU.max))
                swap(c, 3, mx[:, 1], mx[:, 0])
                v.tensor_scalar(nbias[:, :, :, :], mx[:, :, :, :], -QK_SCALE, None, ALU.mult).then_inc(nb_done, 1)
                lo(c, k + 6, units[k + 6])
                lo(c, k + 7, units[k + 7])

                def gate_of(j):
                    dve.wait_ge(zt, c("zt", j + 1))
                    v.scalar_tensor_tensor(out=gate2[:, j, :], in0=scr[:, j, :], scalar=1.0, in1=PJ[(t + 12 + j) % 4][:, :],
                                           op0=ALU.add, op1=ALU.mult).then_inc(pj_fd, 1)

                gate_of(0)
                lo(c, k + 8, units[k + 8])
                dve.wait_ge(ex_done, c("ex", 1))
                swap(c, 4, xch[:, 0], lsum[:, 1])
                link(c, 5, v.tensor_tensor(lsum[:, 0], lsum[:, 0], xch[:, 0], ALU.add))
                swap(c, 6, lsum[:, 1], lsum[:, 0])
                link(c, 7, v.tensor_scalar(lsum[:, :, :, :], lsum[:, :, :, :], 2.0, None, ALU.mult))
                link(c, 8, v.reciprocal(rinv[:, :, :, :], lsum[:, :, :, :]))
                gate_of(1)
                for j in range(2):
                    for b in range(NB):
                        w = slice(max(256 * b - 128, 0), 256 * b + 128)
                        v.tensor_scalar(s0[:, j, w], s0[:, j, w], rinv[:, 0, j, b:b + 1], None, ALU.mult)
                        ins = v.tensor_scalar(s12[j][:, b, :], s12[j][:, b, :], rinv[:, 1, j, b:b + 1], None, ALU.mult)
                ins.then_inc(nrm_done, 1)

            def slopes(n, j):
                return cst[:, bass.ds(n * 2 + (C_SLOPE + j), 1)]

            def probs_out(c):
                for t in range(1, 8, 2):
                    w = 512 if t < 7 else 256
                    dve.wait_ge(at_full, c("at_full", t + 1))
                    nc.vector.tensor_copy(pT[:, 4 * t:4 * t + w // P, :].rearrange("p a b -> p (a b)"),
                                          AT[c.parity("at_slots", t, 4)][:, 0:w]).then_inc(at_fd, 1)

            batch(0, Span(B_FIRST, FIRST), True, batch_units(1, False)[0])
            turns(dve, 1, BATCHES - 1, B_BATCH, BATCH,
                  lambda n, c: batch(n, c, nxt=batch_units(n + 1, False)[0]))
            batch(BATCHES - 1, Span(B_FINAL, BATCH), nxt=LAST_OUT)
            c = Span(B_TAIL, TAIL)
            probs_out(c)
            attended(c)
            dve.wait_ge(fn_in, 16)
            for b in range(NB):
                add_out(c, 0, 0, 2 * b, 2 * b + 2)
                dve.wait_ge(pj_fd, c("pj_fd", 2 * b + 2))
                nc.vector.tensor_tensor(xg[:, b, :], x1[:, b, :], fnorm, ALU.mult).then_inc(xg_done, 1)
            dve.wait_ge(sq_done, 3 * NB)
            inverse_root(c, 0, DM)
            dve.wait_ge(xg_done, NB)
            for b in (0, 2):
                nc.vector.tensor_scalar(xg[:, b, :], xg[:, b, :], rstd[:, b:b + 1], None, ALU.mult).then_inc(y_done[b], 1)

        @block.tensor
        def _(pe):
            def ring(c, plan, name, t, banks, fa, fd, fan, fdn, tail):
                p = t - 4
                while p >= 0 and plan[p] is None:
                    p -= 4
                for who, s, sn in (("A", fa, fan), ("D", fd, fdn)):
                    if p < 0 and tail is not None:
                        if tail[p] == who:
                            pe.wait_ge(s, c(sn, -tail[p:].count(who) + 1))
                    elif p >= 0:
                        if plan[p] == who:
                            pe.wait_ge(s, c(sn, plan[:p + 1].count(who)))
                    else:
                        w = c(sn, 0)
                        if not isinstance(w, int) or w:
                            pe.wait_ge(s, w)
                return banks[c.parity(name, t, 4)]

            def pj(c, plan, t):
                tail = BY_BATCH if c.before.get("nb", 0) else ALL_D
                return ring(c, plan, "pj_slots", t, PJ, pj_fa, pj_fd, "pj_fa", "pj_fd", tail)

            def att(c, plan, t):
                return ring(c, plan, "at_slots", t, AT, at_fa, at_fd, "at_fa", "at_fd", None)

            def product(out_ap, stat_, mov, start, stop):
                for i, (a, b) in enumerate(((0, 0), (0, 1), (1, 0))):
                    ins = nc.tensor.matmul(out_ap, stat_[a], mov[b], start=start and i == 0, stop=stop and i == 2)
                return ins

            def weights(c, k, unit):
                slot = c.parity("unit", k, 2)
                return [unit_view(t[slot], unit) for t in (whi, wlo)]

            def split(c, k, m):
                pe.wait_ge(lo_done, c("halves", 2 * k + m + 1))

            def features_out(c, plan, k, unit, tile):
                w = weights(c, k, unit)
                for m in range(unit[2] // P):
                    o = pj(c, plan, tile + m)
                    for kk in range(KC):
                        if m == 0 and kk % (KC // 2) == 0:
                            split(c, k, kk // (KC // 2))
                        ins = product(o[:, :], [x_[:, kk, m * P:(m + 1) * P] for x_ in w],
                                      [t[:, kk, :] for t in hT], kk == 0, kk == KC - 1)
                    ins.then_inc(pj_full, 1)
                return ins

            def tokens_out(c, plan, k, unit, tile, pick, midway=None):
                w = weights(c, k, unit)
                for s in range(NB):
                    if s % 2 == 0:
                        o = pj(c, plan, tile + s // 2)
                    for kk in range(KC):
                        if s == 0 and kk % (KC // 2) == 0:
                            split(c, k, kk // (KC // 2))
                        ins = product(o[:, (s % 2) * UW:(s % 2 + 1) * UW], [pick(t, kk, s) for t in hT],
                                      [x_[:, kk, :] for x_ in w], kk == 0, kk == KC - 1)
                    if s % 2 == 1:
                        ins.then_inc(pj_full, 1)
                    if s == 1 and midway:
                        midway()

            def out_proj(c, plan, k, unit, tile, o_parts, c0):
                w = weights(c, k, unit)
                for t in range(8):
                    s, nh = t // 2, t % 2
                    o = pj(c, plan, tile + t)
                    for cc in range(2):
                        if t == 0:
                            split(c, k, cc)
                        ins = product(o[:, :], [x_[:, c0 + cc, s * P:(s + 1) * P] for x_ in o_parts],
                                      [x_[:, cc, nh * 512:(nh + 1) * 512] for x_ in w], cc == 0, cc == 1)
                    ins.then_inc(pj_full, 1)

            def block_of(t, kk, s):
                return t[:, kk, s * P:(s + 1) * P]

            def class_of(t, kk, s):
                return t[:, kk, s:SEQ:4]

            def rows_transposed(c, plan, done):
                for k in range(KC):
                    o = att(c, plan, k)
                    if k == 0:
                        pe.wait_ge(xn_done, done)
                    for b in range(NB):
                        ins = nc.tensor.transpose(o[:, b * P:(b + 1) * P], big[:, b, k * P:(k + 1) * P], ident)
                    ins.then_inc(at_full, 1)

            c = Span(B_PRO, PRO)
            pe.wait_ge(c_in, 16)
            rows_transposed(c, AT_PRO, NB)
            pe.wait_ge(lr_split, 1)
            pe.wait_ge(at_fd, KC)
            o = att(c, AT_PRO, KC)
            for kk in range(KC):
                ins = product(o[0:RANK, :], [t[:, kk, :] for t in lr_w], [t[:, kk, :] for t in hT], kk == 0, kk == KC - 1)
            ins.then_inc(at_full, 1)
            features_out(c, PJ_PRO, 0, FIRST_QK[0], 0)
            pe.wait_ge(at_fd, KC + 1)
            pe.wait_ge(lr_in, 48)
            for b in range(NB):
                o = att(c, AT_PRO, KC + 1 + b)
                nc.tensor.matmul(o[:, :], lrT[0:RANK + 1, b * P:(b + 1) * P], wup[0:RANK + 1, :],
                                 start=True, stop=True).then_inc(at_full, 1)
            features_out(c, PJ_PRO, 1, FIRST_QK[1], 2)
            pe.wait_ge(at_fd, KC + 5)
            for h in range(GH):
                o = att(c, AT_PRO, KC + 5 + h)
                for b in range(NB):
                    ins = nc.tensor.matmul(o[:, b * P:(b + 1) * P], lgate[:, b, h * P:(h + 1) * P], tri,
                                           start=True, stop=True)
                ins.then_inc(at_full, 1)

            def head(h, c, last=False):
                units = head_units(h, last)
                plan = PJ_LAST if last else PJ_HEAD

                def level(i):
                    o = att(c, AT_HEAD, i)
                    if i < NL:
                        pe.wait_ge(lvq, c("lvq", i + 1))
                    src = qkd[:, i % 2, :, :] if i < NL else qk
                    for b in range(NB):
                        w = slice(b * P, (b + 1) * P)
                        ins = nc.tensor.matmul(o[:, w], src[:, 1, w], src[:, 0, w], start=True, stop=True)
                    ins.then_inc(at_full, 1)

                pe.wait_ge(pj_fa, c("pj_fa", 0))
                tokens_out(c, plan, 0, units[0], 0, block_of)
                level(0)
                level(1)
                tokens_out(c, plan, 1, units[1], 2, block_of, lambda: level(2))
                level(3)
                tokens_out(c, plan, 2, units[2], 4, block_of, lambda: (level(4), level(5)))
                level(6)
                level(7)
                pe.wait_ge(qd_done, c("qd", 1))
                o = att(c, AT_HEAD, NL + 1)
                nc.tensor.matmul(o[:, 0:128], kd[:, 0, :], qd[:, 0, :], start=True, stop=True)
                nc.tensor.matmul(o[:, 128:384], kd[:, 3, :], qd[:, 1:3, :].rearrange("p a b -> p (a b)"),
                                 start=True, stop=True).then_inc(at_full, 1)
                o = att(c, AT_HEAD, NL + 2)
                nc.tensor.matmul(o[:, 0:256], kd[:, 1, :], qd[:, 1:3, :].rearrange("p a b -> p (a b)"),
                                 start=True, stop=True)
                nc.tensor.matmul(o[:, 256:384], kd[:, 2, :], qd[:, 3, :], start=True, stop=True).then_inc(at_full, 1)
                tokens_out(c, plan, 3, units[3], 6, block_of)
                pe.wait_ge(ats, c("ats", 1))
                pe.wait_ge(at_fd, c("at_fd", NL + 3))
                pe.wait_ge(pj_fd, c("pj_fd", 4))
                between = {(0, 1): 4, (0, 2): 5, (0, 3): 6, (1, 2): 7, (1, 3): 8, (2, 3): 9}
                for i in range(NB):
                    o = att(c, AT_HEAD, NL + 3 + i)
                    for j in range(i + 1):
                        k = i if j == i else between[j, i]
                        ins = product(o[:, :], [t[:, k, :] for t in at], [t[:, j, :] for t in vr], j == 0, j == i)
                    ins.then_inc(at_full, 1)
                k = 4
                if not last:
                    features_out(c, plan, 4, units[4], 8)
                    features_out(c, plan, 5, units[5], 10)
                    k = 6
                pe.wait_ge(at_fd, c("at_fd", NL + 7))
                for i in range(4):
                    o = att(c, AT_HEAD, NL + 7 + i)
                    for b in range(NB):
                        ins = nc.tensor.transpose(o[:, b * P:(b + 1) * P], gate[:, b, i * P:(i + 1) * P], ident)
                    ins.then_inc(at_full, 1)
                pe.wait_ge(at_fd, c("at_fd", NL + 9))
                tile = 8 if last else 12
                out_proj(c, plan, k, units[k], tile, oT, 0)
                pe.wait_ge(at_fd, c("at_fd", NL + 11))
                out_proj(c, plan, k + 1, units[k + 1], tile + 8, oT, 2)

            turns(pe, 0, GH - 1, B_HEAD, HEAD, head)
            head(GH - 1, Span(B_LAST, LAST), True)
            rows_transposed(Span(B_MID, MID), AT_MID, 2 * NB)
            pe.wait_ge(at_fd, B_FIRST["at_fd"])

            def turned(c, plan):
                blocks = []
                for j in range(2):
                    blocks += [s0[:, j, b * P:(b + 1) * P] for b in range(7)]
                    blocks += [s12[j][:, r, g * P:(g + 1) * P] for r in range(4) for g in range(2)]
                pe.wait_ge(nrm_done, c("nrm", 0))
                for t in range(8):
                    o = att(c, plan, t)
                    for i, p in enumerate(blocks[4 * t:4 * t + 4]):
                        ins = nc.tensor.transpose(o[:, i * P:(i + 1) * P], p, ident)
                    ins.then_inc(at_full, 1)

            def attend(c, plan):
                pe.wait_ge(at_fa, c("at_fa", 4))
                pe.wait_ge(at_fd, c("at_fd", 4))
                for j in range(2):
                    w = slice(j * P, (j + 1) * P)
                    o = att(c, plan, 8 + 2 * j)
                    for b in range(NB):
                        d = o[:, b * P:(b + 1) * P]
                        if b:
                            nc.tensor.matmul(d, vv[0][:, b - 1, w], pT[:, 15 * j + 2 * b - 1, :], start=True, stop=False)
                        ins = nc.tensor.matmul(d, vv[0][:, b, w], pT[:, 15 * j + 2 * b, :], start=b == 0, stop=True)
                    ins.then_inc(at_full, 1)
                    o = att(c, plan, 9 + 2 * j)
                    for r in range(4):
                        d = o[:, r * P:(r + 1) * P]
                        for g in range(2):
                            ins = nc.tensor.matmul(d, vv[1 + g][:, r, w], pT[:, 15 * j + 7 + 2 * r + g, :],
                                                   start=g == 0, stop=g == 1)
                    ins.then_inc(at_full, 1)

            def batch(n, c, first=False):
                units = batch_units(n, first)
                pj_plan, at_plan = (PJ_FIRST, AT_FIRST) if first else (PJ_BATCH, AT_BATCH)
                a0 = 0 if first else 12

                def scores(g):
                    q, k = qT[g % 2], kT[g % 2]
                    pe.wait_ge(pj_fa, c("pj_fa", 4 * g + 4))
                    for j in range(2):
                        if g == 0:
                            for half in range(2):
                                o = att(c, at_plan, a0 + 2 * j + half)
                                for b in (2 * half, 2 * half + 1):
                                    kw = slice(max(b - 1, 0) * P, (b + 1) * P)
                                    at0 = (0, 128, 0, 256)[b]
                                    ins = nc.tensor.matmul(o[:, at0:at0 + kw.stop - kw.start], q[:, j, b * P:(b + 1) * P],
                                                           k[:, j, kw], start=True, stop=True)
                                ins.then_inc(at_full, 1)
                        else:
                            o = att(c, at_plan, a0 + 2 + 2 * g + j)
                            for r in range(4):
                                w = slice(r * P, (r + 1) * P)
                                ins = nc.tensor.matmul(o[:, w], q[:, j, w], k[:, j, w], start=True, stop=True)
                            ins.then_inc(at_full, 1)

                features_out(c, pj_plan, 0, units[0], 0)
                if not first:
                    turned(c, at_plan)
                features_out(c, pj_plan, 1, units[1], 2)
                if not first:
                    attend(c, at_plan)
                features_out(c, pj_plan, 2, units[2], 4)
                scores(0)
                k, t = 3, 6
                if not first:
                    pe.wait_ge(ot2, c("ot2", 2))
                    out_proj(c, pj_plan, 3, units[3], 6, oT2, 0)
                    k, t = 4, 14
                features_out(c, pj_plan, k, units[k], t)
                features_out(c, pj_plan, k + 1, units[k + 1], t + 2)
                scores(1)
                features_out(c, pj_plan, k + 2, units[k + 2], t + 4)
                tokens_out(c, pj_plan, k + 3, units[k + 3], t + 6, block_of)
                scores(2)
                tokens_out(c, pj_plan, k + 4, units[k + 4], t + 8, class_of)
                tokens_out(c, pj_plan, k + 5, units[k + 5], t + 10, class_of)
                features_out(c, pj_plan, k + 6, units[k + 6], t + 12)
                features_out(c, pj_plan, k + 7, units[k + 7], t + 13)

            batch(0, Span(B_FIRST, FIRST), True)
            turns(pe, 1, BATCHES - 1, B_BATCH, BATCH, batch)
            batch(BATCHES - 1, Span(B_FINAL, BATCH))
            c = Span(B_TAIL, TAIL)
            turned(c, AT_BATCH)
            attend(c, AT_BATCH)
            pe.wait_ge(ot2, c("ot2", 2))
            out_proj(c, ["D"] * 8, 0, LAST_OUT, 0, oT2, 0)


def constants():
    import numpy as np
    t = np.zeros((P, C_END), np.float32)
    i = np.arange(P)
    t[:, C_ID:C_ID + P] = np.eye(P)
    t[:, C_TRI:C_TRI + P] = np.where(i[:, None] <= i[None, :], 1 / 16.0, 0.0)
    tok = 4 * (i % 32) + i // 32
    own = tok[:, None] - i[None, :]
    cls = i[:, None] - i[None, :]
    far = 1e30
    step = 2.0 ** (-8.0 / GROUPS)
    t[:, C_DIST:C_DIST + 128] = np.where(own <= 0, own + 128.0, far)
    t[:, C_DIST + 128:C_DIST + 256] = np.where(own >= 0, own * 1.0, far)
    t[:, C_DIST + 256:C_DIST + 384] = np.where(cls >= 0, cls * 4.0 * step, far)
    t[:, C_DIST + 384:C_DIST + 512] = np.where((cls >= 0) & (cls % 4 == 0), cls * 4.0 * step ** 2, far)
    s, u = i[:, None], i[None, :]
    for k, L in enumerate(LEVELS):
        pair = (s // (2 * L) == u // (2 * L)) & (s % (2 * L) < L) & (u % (2 * L) >= L)
        t[:, C_MASK + k * P:C_MASK + (k + 1) * P] = pair
    t[:, C_MASK + NL * P:C_MASK + (NL + 1) * P] = np.eye(P)
    h = np.arange(HEADS)
    t[:, C_SLOPE:C_SLOPE + HEADS] = -(2.0 ** (-8.0 * (h + 1) / (GROUPS * HEADS))) / QK_SCALE
    return t


def kernel(x, a_norm, a_w_in, a_w_gate_up, a_b_gate, a_g_out, a_w_out, kv_norm, w_kv, b_norm, b_w_in, b_w_out,
           final_norm):
    import numpy as np
    import concourse.bacc as bacc
    from concourse.bass_utils import run_bass_kernel_spmd

    a = {n: np.ascontiguousarray(v) for n, v in dict(
        x=x[0], a_w_in=a_w_in[0], w_gate_up=np.concatenate([a_w_gate_up[0], a_b_gate[0:1]], 0), a_w_out=a_w_out[0],
        w_kv=w_kv, b_w_in=b_w_in[0], b_w_out=b_w_out[0],
        gains=np.concatenate([np.asarray(g).reshape(-1, P).T for g in (a_norm[0], kv_norm, b_norm[0], a_g_out[0])], 1),
        final_norm=final_norm, consts=constants()).items()}
    nc = bacc.Bacc("TRN2", target_bir_lowering=False, num_devices=1, dynamic_dma_scratch_size=1024)
    aps = [nc.dram_tensor(f"in_{n}", v.shape, mybir.dt.from_np(v.dtype), kind="ExternalInput").ap() for n, v in a.items()]
    o = nc.dram_tensor("out_y", (SEQ, DM), FP, kind="ExternalOutput").ap()
    trunk(nc, *aps, o)
    r = run_bass_kernel_spmd(nc, [{f"in_{n}": v for n, v in a.items()}], core_ids=[0])
    return r.results[0]["out_y"].reshape(1, SEQ, DM)
```

```python
import concourse.bass as bass
from concourse import mybir
from contextlib import ExitStack

FP = mybir.dt.float32
FR = mybir.dt.float32r
I32 = mybir.dt.int32
ALU = mybir.AluOpType
ACT = mybir.ActivationFunctionType
AX = mybir.AxisListType

P = 128
SEQ, DM, DI = 512, 1024, 2048
NB = SEQ // P
KC = DM // P
EPS = 1e-6
GH, DV, RANK = 4, 512, 16
QK_SCALE = 128.0 ** -0.5
VCOL, ZCOL, LRCOL = DM, DM + DI, DM + 2 * DI
HEADS, GROUPS = 16, 3
UW = 256
UE = KC * UW
LEVELS = (64, 32, 16, 8, 4, 2, 1)
NL = len(LEVELS)
BATCHES = HEADS // 2
C_ID, C_TRI, C_DIST, C_MASK = 0, 128, 256, 768
C_SLOPE = C_MASK + 8 * 128
C_END = C_SLOPE + HEADS
G_A, G_KV, G_B, G_OUT = 0, 8, 16, 24

PJ_PRO, AT_PRO = ["A", None] * 2, ["D"] * 13 + ["A"] * 4
PJ_HEAD, AT_HEAD = ["D"] * 8 + ["A", None] * 2 + ["D"] * 16, ["D"] * 18 + [None] * 2
PJ_LAST = ["D"] * 24
AT_MID = ["D"] * 8
PJ_FIRST, AT_FIRST = ["A"] * 18 + ["D"] * 2, ["D"] * 8
PJ_BATCH, AT_BATCH = ["A"] * 6 + ["D"] * 8 + ["A"] * 12 + ["D"] * 2, ["A", "D"] * 6 + ["D"] * 8
RSQ = 12

ALL_D, BY_BATCH = ["D"] * 4, ["A", "A", "D", "D"]


def adds(pj, at, tiles_of_units, **more):
    ends = [sum(tiles_of_units[:k + 1]) for k in range(len(tiles_of_units))]
    return dict(more, ends=ends, unit=len(ends), halves=2 * len(ends), pj_slots=len(pj), at_slots=len(at),
                pj_full=len(pj) - pj.count(None), pj_fa=pj.count("A"), pj_fd=pj.count("D"),
                at_full=len(at) - at.count(None), at_fa=at.count("A"), at_fd=at.count("D"))


PER_HEAD = dict(dv=RSQ + 3, lvd=NL, lve=NL + 1, lvq=NL, bh=1, at_hi=2, ats=1, qd=1, sq=4, vh=4, th=4, oth=4, og=4, g2=2)
PER_BATCH = dict(dv=9, zt=2, nb=1, ex=1, nrm=1)
PRO = adds(PJ_PRO, AT_PRO, [1, 1], dv=2 * RSQ)
HEAD = adds(PJ_HEAD, AT_HEAD, [2, 2, 2, 2, 1, 1, 8, 8], **PER_HEAD)
LAST = adds(PJ_LAST, AT_HEAD, [2, 2, 2, 2, 8, 8], **PER_HEAD)
MID = adds([], AT_MID, [], dv=2 * RSQ)
FIRST = adds(PJ_FIRST, AT_FIRST, [2] * 9 + [1, 1], **PER_BATCH)
BATCH = adds(PJ_BATCH, AT_BATCH, [2] * 3 + [8] + [2] * 6 + [1, 1], og2=2, ob=2, ot2=2, **PER_BATCH)
FINAL = adds(PJ_FIRST, AT_BATCH, [2] * 9 + [1, 1], og2=2, ob=2, ot2=2, **PER_BATCH)
TAIL = adds(["D"] * 16, AT_BATCH[:12], [8, 8], dv=2 * RSQ)


class Span:

    def __init__(self, before, per, turn=None):
        self.before, self.per, self.turn = before, per, turn

    def __call__(self, name, k):
        v = self.before.get(name, 0) + k
        return v if self.turn is None else self.turn * self.per.get(name, 0) + v

    def loads(self, k):
        v = 16 * ((self.before.get("unit", 0) + k) // 2 + 1)
        return v if self.turn is None else self.turn * (8 * self.per["unit"]) + v

    def parity(self, name, k, ring):
        assert self.turn is None or self.per.get(name, 0) % ring == 0
        return (self.before.get(name, 0) + k) % ring


def after(before, per, turns=1):
    names = (set(before) | set(per)) - {"ends"}
    return {k: before.get(k, 0) + turns * per.get(k, 0) for k in names}


B_PRO = {"pj_fd": 4}
B_HEAD = after(B_PRO, PRO)
B_LAST = after(B_HEAD, HEAD, GH - 1)
B_MID = after(B_LAST, LAST)
B_FIRST = after(B_MID, MID)
B_BATCH = after(B_FIRST, FIRST)
B_FINAL = after(B_BATCH, BATCH, BATCHES - 2)
B_TAIL = after(B_FINAL, FINAL)


def trunk(nc, x, a_w_in, w_gate_up, a_w_out, w_kv, b_w_in, b_w_out, gains, final_norm, consts, out):
    ctx = ExitStack()
    with ctx:
        def sb(name, shape, dt=FP):
            return ctx.enter_context(nc.sbuf_tensor(name, shape, dt))

        def sem(name):
            return ctx.enter_context(nc.semaphore(name))

        cst = sb("cst", [P, C_END])
        gain = sb("gain", [P, 28])
        x1 = sb("x1", [P, NB, DM])
        big = sb("big", [P, NB, DM])
        hT = [sb(f"hT_{s}", [P, KC, SEQ], FR) for s in ("hi", "lo")]
        raw = [sb(f"raw{i}", [P, UE]) for i in range(2)]
        whi = [sb(f"whi{i}", [P, UE], FR) for i in range(2)]
        wlo = [sb(f"wlo{i}", [P, UE], FR) for i in range(2)]
        small = sb("small", [P, 96])
        ss, var, rstd, nwt = (small[:, 4 * i:4 * i + 4] for i in range(4))
        scr = sb("scr", [P, 2, 512])
        arena = sb("arena", [P, 13824])
        arena_r = sb("arena_r", [P, 11008], FR)

        def cut(t, at, *shape):
            n = 1
            for d in shape:
                n *= d
            v = t[:, at:at + n]
            if len(shape) == 2:
                v = v.rearrange("p (a b) -> p a b", a=shape[0])
            if len(shape) == 3:
                v = v.rearrange("p (a b c) -> p a b c", a=shape[0], b=shape[1])
            return v

        ident = cst[:, C_ID:C_ID + P]
        tri = cst[:, C_TRI:C_TRI + P]
        bT = cut(arena, 0, GH, SEQ)
        qk = cut(arena, 2048, 2, SEQ)
        ee = cut(arena, 3072, 2, SEQ)
        qkd = cut(arena, 4096, 2, SEQ)
        atd = cut(arena, 6144, NB, P)
        e1 = cut(arena, 6656, 3, P)
        e2 = cut(arena, 7040, 3, P)
        qd = cut(arena, 7424, 4, P)
        kd = cut(arena, 7936, 4, P)
        gate = big[:, 0:2, :].rearrange("p a (b c) -> p (a b) c", b=2)
        lgate = big[:, 2:4, :].rearrange("p a (b c) -> p (a b) c", b=2)
        lrT = arena[:, 8512:9024]
        wup = arena[:, 9024:9536]
        raw_lr = cut(arena, 9536, KC, RANK)
        etot = arena[:, 9664:9668]
        bh = arena[:, 9668:10180]
        tick = arena[:, 10180:10181]
        at = [cut(arena_r, 0, 10, P), cut(arena_r, 1280, 10, P)]
        lr_w = [cut(arena_r, 2560, KC, RANK), cut(arena_r, 2688, KC, RANK)]
        vr = [cut(arena_r, 6912, NB, DV), cut(arena_r, 8960, NB, DV)]
        oT = [cut(arena_r, 2816, NB, SEQ), cut(arena_r, 4864, NB, SEQ)]
        qT = [cut(arena, 1024 * i, 2, SEQ) for i in range(2)]
        kT = [cut(arena, 2048, 2, SEQ), big[:, 3, :].rearrange("p (j t) -> p j t", j=2)]
        vv = [cut(arena, 3072 + 1024 * g, NB, UW) for g in range(GROUPS)]
        s0 = cut(arena, 6144, 2, 896)
        s12 = [cut(arena, 7936 + 1024 * j, NB, 256) for j in range(2)]
        pT = cut(arena, 9984, 30, P)
        gate2 = big[:, 2, :].rearrange("p (j t) -> p j t", j=2)
        o_sum = big[:, 0, :].rearrange("p (j t) -> p j t", j=2)
        oT2 = [cut(arena_r, 1024 * i, 2, SEQ) for i in range(2)]
        oT2_last = [cut(arena_r, 2048 + 1024 * i, 2, SEQ) for i in range(2)]
        fnorm = big[:, 1, :]
        xg = cut(arena, 0, NB, DM)

        def stat(k):
            return small[:, 16 + 16 * k:32 + 16 * k].rearrange("p (l j b) -> p l j b", l=2, j=2)

        mx, nbias, lsum, rinv, xch = (stat(k) for k in range(5))
        PJ = [ctx.enter_context(nc.psum_tensor(f"PJ{i}", [P, 512], FP)) for i in range(4)]
        AT = [ctx.enter_context(nc.psum_tensor(f"AT{i}", [P, 512], FP)) for i in range(4)]

        raw_full = [sem("raw_full0"), sem("raw_full1")]
        hi_done, lo_done = sem("hi_done"), sem("lo_done")
        pj_full, pj_fa, pj_fd = sem("pj_full"), sem("pj_fa"), sem("pj_fd")
        at_full, at_fa, at_fd = sem("at_full"), sem("at_fa"), sem("at_fd")
        dv = sem("dv")
        x_in = [sem(f"x_in{b}") for b in range(NB)]
        c_in, m_in, lr_in, wup_in, fn_in = (sem(n) for n in ("c_in", "m_in", "lr_in", "wup_in", "fn_in"))
        sq_done, ht_hi = sem("sq_done"), sem("ht_hi")
        xn_a, xn_d = sem("xn_a"), sem("xn_d")
        lr_hi, lr_split = sem("lr_hi"), sem("lr_split")
        ones_set = sem("ones_set")
        u_abs, u_exp, u_ln = sem("u_abs"), sem("u_exp"), sem("u_ln")
        y_done, xg_done, out_done = [sem(f"y_done{b}") for b in range(NB)], sem("xg_done"), sem("out_done")
        bh_done, lvd, lve, lvq, at_hi, ats = (sem(n) for n in ("bh_done", "lvd", "lve", "lvq", "at_hi", "ats"))
        qd_done, head_sq, vh, th, oth = (sem(n) for n in ("qd_done", "head_sq", "vh", "th", "oth"))
        og, g2 = sem("og"), sem("g2")
        nb_done, ex_done, nrm_done, zt = (sem(n) for n in ("nb_done", "ex_done", "nrm_done", "zt"))
        og2, ob, ot2 = (sem(n) for n in ("og2", "ob", "ot2"))

        def by_rows(w):
            return w.rearrange("(k p) c -> p k c", p=P)

        w_a, w_b, w_s = by_rows(a_w_in), by_rows(b_w_in), by_rows(w_kv)
        o_a, o_b = by_rows(a_w_out), by_rows(b_w_out)

        def in_unit(w, col, cols, g):
            return (w[:, :, bass.ds(col, cols)], KC, cols, g)

        def out_unit(w, row, g):
            return (w[:, bass.ds(row, 2), :], 2, DM, g)

        def v_a(h, u):
            return in_unit(w_a, h * DV + (VCOL + u * UW), UW, G_A)

        def z_a(h, u):
            return in_unit(w_a, h * DV + (ZCOL + u * UW), UW, G_A)

        def qk_a(h, i):
            return in_unit(w_a, h * P + i * GH * P, P, G_A)

        def head_units(h, last):
            mid = [] if last else [qk_a(h + 1, 0), qk_a(h + 1, 1)]
            return ([v_a(h, 0), v_a(h, 1), z_a(h, 0), z_a(h, 1)] + mid
                    + [out_unit(o_a, h * 4 + 2 * u, G_OUT + 2 * u) for u in range(2)])

        def batch_units(n, out):
            u = []
            for g in range(GROUPS):
                u += [in_unit(w_b, n * UW + g * DI, UW, G_B), in_unit(w_s, n * UW + g * DI, UW, G_KV)]
            u += [in_unit(w_s, n * UW + (GROUPS + g) * DI, UW, G_KV) for g in range(GROUPS)]
            u += [in_unit(w_b, n * UW + (GROUPS * DI + j * P), P, G_B) for j in range(2)]
            return u[:3] + [out_unit(o_b, n * 2 + (-2), None)] + u[3:] if out else u

        FIRST_QK = [qk_a(0, 0), qk_a(0, 1)]
        FIRST_UNITS = batch_units(0, False)
        FIRST_UNITS = FIRST_UNITS[6:7] + FIRST_UNITS[:6] + FIRST_UNITS[7:]
        TAIL_OUT = [out_unit(o_b, HEADS - 4, None), out_unit(o_b, HEADS - 2, None)]

        def unit_view(t, unit):
            _, k, cols, _ = unit
            return t[:, 0:k * cols].rearrange("p (k c) -> p k c", k=k)

        def turns(eng, lo, hi, before, per, body):
            with eng.Fori(0, hi - lo) as i:
                body(i + lo, Span(before, per, i))

        block = ctx.enter_context(nc.Block())

        @block.sync
        def _(sp):
            def load(c, k, unit):
                u = c("unit", k)
                slot = c.parity("unit", k, 2)
                if not isinstance(u, int) or u >= 2:
                    sp.wait_ge(lo_done, c("halves", 2 * k - 2))
                sp.dma_start(unit_view(raw[slot], unit), unit[0]).then_inc(raw_full[slot], 16)

            sp.dma_start(gain[:, :], gains).then_inc(lr_in, 16)
            sp.dma_start(raw_lr[:, :, :], w_a[:, :, LRCOL:LRCOL + RANK]).then_inc(lr_in, 16)
            for b in range(NB):
                sp.dma_start(x1[:, b, :], x[b * P:(b + 1) * P, :]).then_inc(x_in[b], 16)
                if b == 0:
                    sp.dma_start(cst[:, 0:C_DIST], consts[:, 0:C_DIST]).then_inc(c_in, 16)
            sp.dma_start(wup[0:RANK + 1, :], w_gate_up).then_inc(wup_in, 16)
            c = Span(B_PRO, PRO)
            for k, unit in enumerate(FIRST_QK):
                load(c, k, unit)
            sp.dma_start(cst[:, C_DIST:C_END], consts[:, C_DIST:C_END]).then_inc(m_in, 16)

            def head(h, c, last=False):
                for k, unit in enumerate(head_units(h, last)):
                    load(c, k, unit)

            turns(sp, 0, GH - 1, B_HEAD, HEAD, head)
            head(GH - 1, Span(B_LAST, LAST), True)

            def batch(n, c, out=True):
                for k, unit in enumerate(batch_units(n, out)):
                    load(c, k, unit)

            for k, unit in enumerate(FIRST_UNITS):
                load(Span(B_FIRST, FIRST), k, unit)
            turns(sp, 1, BATCHES - 1, B_BATCH, BATCH, batch)
            batch(BATCHES - 1, Span(B_FINAL, FINAL), False)
            for k, unit in enumerate(TAIL_OUT):
                load(Span(B_TAIL, TAIL), k, unit)
            sp.wait_ge(at_fd, B_FIRST["at_fd"])
            sp.dma_start(fnorm, final_norm.rearrange("(a n) -> a n", a=1).to_broadcast([P, DM])).then_inc(fn_in, 16)
            for b in range(NB):
                sp.wait_ge(y_done[b], 1)
                sp.dma_start(out[b * P:(b + 1) * P, :], xg[:, b, :]).then_inc(out_done, 16)
            sp.wait_ge(out_done, 64)

        @block.gpsimd
        def _(pool):
            pool.memset(lrT[0:32, :], 1.0).then_inc(ones_set, 1)

            def head(h, c):
                pool.wait_ge(bh_done, c("bh", 1))
                for i, L in enumerate(LEVELS):
                    v = bh[:, :].rearrange("p (n u l) -> p n u l", u=2, l=L)
                    d = ee[:, i % 2, :].rearrange("p (n u l) -> p n u l", u=2, l=L)
                    ref = v[:, :, 0, L - 1:L].to_broadcast([P, SEQ // (2 * L), L])
                    w = c("lvq", max(i - 1, 0))
                    if not isinstance(w, int) or w:
                        pool.wait_ge(lvq, w)
                    pool.tensor_tensor(d[:, :, 0, :], ref, v[:, :, 0, :], ALU.subtract)
                    pool.tensor_tensor(d[:, :, 1, :], v[:, :, 1, :], ref, ALU.subtract).then_inc(lvd, 1)

            turns(pool, 0, GH - 1, B_HEAD, HEAD, head)
            head(GH - 1, Span(B_LAST, LAST))
            c = Span(B_TAIL, TAIL)
            pool.wait_ge(fn_in, 16)
            for b in range(NB):
                pool.wait_ge(pj_fd, c("pj_fd", 2 * b + 10))
                pool.tensor_tensor(xg[:, b, :], x1[:, b, :], fnorm, ALU.mult).then_inc(xg_done, 1)

        @block.scalar
        def _(act):
            def hi(c, k, unit):
                slot = c.parity("unit", k, 2)
                u = c("unit", k)
                act.wait_ge(raw_full[slot], c.loads(k))
                if not isinstance(u, int) or u >= 2:
                    act.wait_ge(pj_full, c("pj_full", c.per["ends"][k - 2] if k >= 2 else 0))
                src, dst = unit_view(raw[slot], unit), unit_view(whi[slot], unit)
                half = unit[1] // 2
                for m in range(2):
                    if unit[3] is None:
                        nc.scalar.activation(dst[:, m, :], src[:, m, :], ACT.Copy).then_inc(hi_done, 1)
                        continue
                    for j in range(m * half, (m + 1) * half):
                        ins = nc.scalar.activation(dst[:, j, :], src[:, j, :], ACT.Copy,
                                                   scale=gain[:, unit[3] + j:unit[3] + j + 1])
                    ins.then_inc(hi_done, 1)

            def squares(blocks, done, added=None):
                for b in blocks:
                    if added is None:
                        act.wait_ge(x_in[b], 16)
                    else:
                        act.wait_ge(pj_fd, added - 6 + 2 * b)
                    if b:
                        act.wait_ge(sq_done, done + b)
                    nc.scalar.activation(scr[:, :, :].rearrange("p a b -> p (a b)"), x1[:, b, :], ACT.Square,
                                         accum_out=ss[:, b:b + 1]).then_inc(sq_done, 1)

            def transposed(c, p):
                for k in range(4):
                    act.wait_ge(at_full, c("at_full", 4 * p + k + 1))
                    nc.scalar.activation(hT[0][:, 2 * k:2 * k + 2, 256 * p:256 * p + 256],
                                         AT[c.parity("at_slots", 4 * p + k, 4)][:, :].rearrange("p (c t) -> p c t", c=2),
                                         ACT.Copy).then_inc(ht_hi, 1)

            def normalised(c, p):
                b = 2 * p + 1
                act.wait_ge(dv, c("dv", RSQ * (p + 1)))
                nc.scalar.activation(big[:, b, :], x1[:, b, :], ACT.Copy, scale=rstd[:, b:b + 1]).then_inc(xn_a, 1)

            c = Span(B_PRO, PRO)
            squares(range(NB), 0)
            normalised(c, 0)
            normalised(c, 1)
            transposed(c, 0)
            transposed(c, 1)
            hi(c, 0, FIRST_QK[0])
            hi(c, 1, FIRST_QK[1])
            for b in range(NB):
                act.wait_ge(u_abs, b + 1)
                nc.scalar.activation(gate[:, b, :], gate[:, b, :], ACT.Exp, scale=-1.0).then_inc(u_exp, 1)
            for b in range(NB):
                act.wait_ge(u_exp, b + 1)
                nc.scalar.activation(lgate[:, b, :], gate[:, b, :], ACT.Ln, bias=1.0).then_inc(u_ln, 1)
            def q_or_k(c, i, tile, pj_index):
                act.wait_ge(pj_full, c("pj_full", pj_index + 1))
                nc.scalar.activation(qk[:, i, :], PJ[tile % 4][:, :], ACT.Copy,
                                     scale=QK_SCALE if i == 0 else 1.0).then_inc(pj_fa, 1)

            hi(c, 2, v_a(0, 0))
            for i in range(2):
                q_or_k(c, i, 2 * i, i)
            for h in range(GH):
                act.wait_ge(at_full, KC + 6 + h)
                nc.scalar.activation(bT[:, h, :], AT[(KC + 5 + h) % 4][:, :], ACT.Copy).then_inc(at_fa, 1)

            def head(h, c, last=False, nxt=None):
                units = head_units(h, last) + [nxt(h)]
                b = bh[:, :].rearrange("p (n t) -> p n t", t=P)

                def value_hi(u):
                    for i in range(2):
                        t = 2 * u + i
                        act.wait_ge(pj_full, c("pj_full", t + 1))
                        nc.scalar.activation(vr[0][:, 2 * i:2 * i + 2, u * UW:(u + 1) * UW],
                                             PJ[t % 4][:, :].rearrange("p (s c) -> p s c", s=2),
                                             ACT.Copy).then_inc(vh, 1)

                def tanh(u, i):
                    t = 4 + 2 * u + i
                    act.wait_ge(pj_full, c("pj_full", t + 1))
                    if u:
                        act.wait_ge(pj_fd, c("pj_fd", t - 1))
                        act.wait_ge(head_sq, c("sq", 4))
                    else:
                        w = c("g2", 0)
                        if not isinstance(w, int) or w:
                            act.wait_ge(g2, w)
                    nc.scalar.activation(scr[:, i, :], PJ[t % 4][:, :], ACT.Tanh, scale=0.5).then_inc(th, 1)

                def oT_hi(i):
                    act.wait_ge(at_full, c("at_full", NL + 8 + i))
                    nc.scalar.activation(oT[0][:, i, :], AT[c.parity("at_slots", NL + 7 + i, 4)][:, :],
                                         ACT.Copy).then_inc(oth, 1)

                def exps(lo, up):
                    for i in range(lo, up):
                        act.wait_ge(lvd, c("lvd", i + 1))
                        nc.scalar.activation(ee[:, i % 2, :], ee[:, i % 2, :], ACT.Exp).then_inc(lve, 1)

                act.wait_ge(at_fa, c("at_fa", 0))
                w = c("lvq", 0)
                if not isinstance(w, int) or w:
                    act.wait_ge(lvd, c("lvd", 0))
                nc.scalar.activation(bh[:, :].unsqueeze(1), bT[:, bass.ds(h, 1), :], ACT.Copy).then_inc(bh_done, 1)
                exps(0, 2)
                hi(c, 1, units[1])
                exps(2, 4)
                value_hi(0)
                hi(c, 2, units[2])
                exps(4, 6)
                nc.scalar.activation(e1[:, :, :], b[:, 1:4, :], ACT.Exp)
                nc.scalar.activation(etot, b[:, :, P - 1], ACT.Exp)
                for s in range(3):
                    ins = nc.scalar.activation(e2[:, s, :], b[:, s, :], ACT.Exp, scale=-1.0, bias=b[:, s, P - 1:P])
                ins.then_inc(lve, 1)
                exps(NL - 1, NL)
                value_hi(1)
                hi(c, 3, units[3])
                act.wait_ge(at_fd, c("at_fd", NL + 1))
                nc.scalar.activation(at[0][:, 0:4, :], atd[:, :, :], ACT.Copy).then_inc(at_hi, 1)
                for i in range(2):
                    act.wait_ge(at_full, c("at_full", NL + 2 + i))
                    ins = nc.scalar.activation(at[0][:, 4 + 3 * i:7 + 3 * i, :].rearrange("p a b -> p (a b)"),
                                               AT[c.parity("at_slots", NL + 1 + i, 4)][:, 0:384], ACT.Copy)
                ins.then_inc(at_hi, 1)
                tanh(0, 0)
                tanh(0, 1)
                hi(c, 4, units[4])
                act.wait_ge(pj_fd, c("pj_fd", 6))
                for i in range(NB):
                    act.wait_ge(at_full, c("at_full", NL + 4 + i))
                    if i >= 2:
                        act.wait_ge(head_sq, c("sq", i - 1))
                    nc.scalar.activation(scr[:, i % 2, :], AT[c.parity("at_slots", NL + 3 + i, 4)][:, :],
                                         ACT.Square, accum_out=ss[:, i:i + 1]).then_inc(head_sq, 1)
                tanh(1, 0)
                if last:
                    oT_hi(0)
                    oT_hi(1)
                tanh(1, 1)
                hi(c, 5, units[5])
                if last:
                    oT_hi(2)
                    oT_hi(3)
                    hi(c, 6, units[6])
                    return
                act.wait_ge(qd_done, c("qd", 1))
                q_or_k(c, 0, 8, 8)
                hi(c, 6, units[6])
                for i in range(4):
                    oT_hi(i)
                q_or_k(c, 1, 10, 9)
                hi(c, 7, units[7])
                hi(c, 8, units[8])

            turns(act, 0, GH - 1, B_HEAD, HEAD, lambda h, c: head(h, c, nxt=lambda h: v_a(h + 1, 0)))
            head(GH - 1, Span(B_LAST, LAST), True, nxt=lambda h: FIRST_UNITS[0])

            c = Span(B_MID, MID)
            squares(range(3), NB, c("pj_fd", 0))
            normalised(c, 0)
            transposed(c, 0)
            squares((3,), NB, c("pj_fd", 0))
            normalised(c, 1)
            transposed(c, 1)

            def batch(n, c, first=False, out=True, nxt=None):
                units = (FIRST_UNITS if first else batch_units(n, out)) + [nxt]
                d = 1 if first else 0

                def copy(tile, dst, src=None):
                    act.wait_ge(pj_full, c("pj_full", tile + 1))
                    bank = PJ[tile % 4][:, :]
                    nc.scalar.activation(dst, bank if src is None else src(bank), ACT.Copy).then_inc(pj_fa, 1)

                def heads(tile, dst, order):
                    for j in range(2):
                        if order == "tokens":
                            copy(tile + j, dst[:, j, :])
                        elif order == "blocks":
                            copy(tile + j, dst[:, j, :].rearrange("p (b r i) -> p b r i", b=NB, r=4),
                                 lambda t: t.rearrange("p (b i r) -> p b r i", b=NB, r=4))
                        else:
                            copy(tile + j, dst[:, j, :].rearrange("p (r j) -> p r j", r=4),
                                 lambda t: t.rearrange("p (j r) -> p r j", r=4))

                def value(g, tile, i):
                    copy(tile + i, vv[g][:, 2 * i:2 * i + 2, :], lambda t: t.rearrange("p (s c) -> p s c", s=2))

                def values(g, tile):
                    value(g, tile, 0)
                    value(g, tile, 1)

                if first:
                    hi(c, 1, units[1])
                    values(0, 0)
                hi(c, 1 + d, units[1 + d])
                if not first:
                    probs_copy(c)
                heads(2 * d, qT[0], "blocks")
                hi(c, 2 + d, units[2 + d])
                heads(2 + 2 * d, kT[0], "tokens")
                if not first:
                    attended_act(c)
                hi(c, 3 + d, units[3 + d])
                heads(4 + 2 * d, qT[1], "classes")
                k, t = 3 + d, 6 + 2 * d
                if out:
                    hi(c, 4, units[4])
                    k, t = 4, 14
                hi(c, k + 1, units[k + 1])
                heads(t, kT[1], "classes")
                hi(c, k + 2, units[k + 2])
                heads(t + 2, qT[0], "classes")
                hi(c, k + 3, units[k + 3])
                heads(t + 4, kT[0], "classes")
                if first:
                    k, t = k - 1, t - 2
                else:
                    hi(c, k + 4, units[k + 4])
                    values(0, t + 6)
                hi(c, k + 5, units[k + 5])
                values(1, t + 8)
                hi(c, k + 6, units[k + 6])
                act.wait_ge(nb_done, c("nb", 1))
                for j in range(2):
                    for b in range(NB):
                        w = slice(max(256 * b - 128, 0), 256 * b + 128)
                        nc.scalar.activation(s0[:, j, w], s0[:, j, w], ACT.Exp, scale=QK_SCALE,
                                             bias=nbias[:, 0, j, b:b + 1], accum_out=lsum[:, 0, j, b:b + 1])
                        ins = nc.scalar.activation(s12[j][:, b, :], s12[j][:, b, :], ACT.Exp, scale=QK_SCALE,
                                                   bias=nbias[:, 1, j, b:b + 1], accum_out=lsum[:, 1, j, b:b + 1])
                    if j == 0:
                        value(2, t + 10, 0)
                ins.then_inc(ex_done, 1)
                value(2, t + 10, 1)
                for j in range(2):
                    hi(c, k + 7 + j, units[k + 7 + j])
                    act.wait_ge(pj_full, c("pj_full", t + 13 + j))
                    nc.scalar.activation(scr[:, j, :], PJ[(t + 12 + j) % 4][:, :], ACT.Tanh, scale=0.5).then_inc(zt, 1)

            def probs_copy(c):
                for t in range(0, 8, 2):
                    act.wait_ge(at_full, c("at_full", t + 1))
                    nc.scalar.activation(pT[:, 4 * t:4 * t + 4, :].rearrange("p a b -> p (a b)"),
                                         AT[c.parity("at_slots", t, 4)][:, :], ACT.Copy).then_inc(at_fa, 1)

            def attended_act(c, dst=oT2):
                for j in range(2):
                    act.wait_ge(at_full, c("at_full", 9 + 2 * j))
                    nc.scalar.activation(o_sum[:, j, :].rearrange("p (b i r) -> p b r i", b=NB, r=4),
                                         AT[c.parity("at_slots", 8 + 2 * j, 4)][:, :].rearrange(
                                             "p (b r i) -> p b r i", b=NB, r=4), ACT.Copy).then_inc(at_fa, 1)
                for j in range(2):
                    act.wait_ge(og2, c("og2", j + 1))
                    nc.scalar.activation(dst[0][:, j, :], o_sum[:, j, :], ACT.Copy).then_inc(ob, 1)

            batch(0, Span(B_FIRST, FIRST), True, False, batch_units(1, True)[0])
            turns(act, 1, BATCHES - 1, B_BATCH, BATCH,
                  lambda n, c: batch(n, c, nxt=batch_units(n + 1, True)[0]))
            batch(BATCHES - 1, Span(B_FINAL, FINAL), out=False, nxt=TAIL_OUT[0])
            c = Span(B_TAIL, TAIL)
            probs_copy(c)
            hi(c, 1, TAIL_OUT[1])
            attended_act(c, oT2_last)
            squares(range(NB), 2 * NB, c("pj_fd", 16))
            for b in (1, 3):
                act.wait_ge(dv, c("dv", RSQ * (1 + b // 2)))
                act.wait_ge(xg_done, b + 1)
                nc.scalar.activation(xg[:, b, :], xg[:, b, :], ACT.Copy, scale=rstd[:, b:b + 1]).then_inc(y_done[b], 1)

        @block.vector
        def _(dve):
            def link(c, k, ins):
                ins.then_inc(dv, 1)
                dve.wait_ge(dv, c("dv", k + 1))

            def lo(c, k, unit, halves=(0, 1)):
                slot = c.parity("unit", k, 2)
                src, h, dst = (unit_view(t[slot], unit) for t in (raw, whi, wlo))
                h = h.bitcast(FP)
                half = unit[1] // 2
                for m in halves:
                    dve.wait_ge(hi_done, c("halves", 2 * k + m + 1))
                    if unit[3] is None:
                        nc.vector.tensor_tensor(dst[:, m, :], src[:, m, :], h[:, m, :], ALU.subtract).then_inc(lo_done, 1)
                        continue
                    for j in range(m * half, (m + 1) * half):
                        ins = nc.vector.scalar_tensor_tensor(out=dst[:, j, :], in0=src[:, j, :],
                                                             scalar=gain[:, unit[3] + j:unit[3] + j + 1],
                                                             in1=h[:, j, :], op0=ALU.mult, op1=ALU.subtract)
                    ins.then_inc(lo_done, 1)

            def root_steps(c, k, width, cols=slice(0, NB), start=0, end=RSQ):
                v = nc.vector
                s_, v_, r_, n_ = (t[:, cols] for t in (ss, var, rstd, nwt))
                for i in range(start, end):
                    if i == 0:
                        ins = v.tensor_scalar(v_, s_, 1.0 / width, EPS, ALU.mult, ALU.add)
                    elif i == 1:
                        ins = v.tensor_scalar(r_.bitcast(I32), v_.bitcast(I32), 1, None, ALU.logical_shift_right)
                    elif i == 2:
                        ins = v.tensor_scalar(r_.bitcast(I32), r_.bitcast(I32), -1.0, float(0x5F3759DF),
                                              ALU.mult, ALU.add)
                    elif i % 3 == 0:
                        ins = v.tensor_tensor(n_, r_, r_, ALU.mult)
                    elif i % 3 == 1:
                        ins = v.scalar_tensor_tensor(out=n_, in0=n_, scalar=-0.5, in1=v_, op0=ALU.mult, op1=ALU.mult)
                    else:
                        ins = v.scalar_tensor_tensor(out=r_, in0=n_, scalar=1.5, in1=r_, op0=ALU.add, op1=ALU.mult)
                    link(c, k + i, ins)

            def add_last(c, count, done):
                for t in range(2):
                    add_out(c, 0, count, 4 + t, 5 + t)
                    if t == 0:
                        dve.wait_ge(sq_done, done - 2)
                    root_steps(c, 0, DM, slice(0, 2), 6 * t, 6 * t + 6)

            def normalised(c, p):
                b = 2 * p
                nc.vector.tensor_scalar(big[:, b, :], x1[:, b, :], rstd[:, b:b + 1], None, ALU.mult).then_inc(xn_d, 1)

            def transposed_lo(c, p, done):
                for k in range(4):
                    dve.wait_ge(ht_hi, done + 4 * p + k + 1)
                    w = (slice(None), slice(2 * k, 2 * k + 2), slice(256 * p, 256 * p + 256))
                    nc.vector.tensor_tensor(hT[1][w], AT[c.parity("at_slots", 4 * p + k, 4)][:, :].rearrange(
                        "p (c t) -> p c t", c=2), hT[0].bitcast(FP)[w], ALU.subtract).then_inc(at_fd, 1)

            nc.vector.memset(tick, 0.0).then_inc(pj_fd, 4)
            c = Span(B_PRO, PRO)
            dve.wait_ge(lr_in, 32)
            for j in range(KC):
                ins = nc.vector.tensor_scalar(lr_w[0][:, j, :], raw_lr[:, j, :], gain[:, j:j + 1], None, ALU.mult)
            ins.then_inc(lr_hi, 1)
            dve.wait_ge(lr_hi, 1)
            for j in range(KC):
                ins = nc.vector.scalar_tensor_tensor(out=lr_w[1][:, j, :], in0=raw_lr[:, j, :], scalar=gain[:, j:j + 1],
                                                     in1=lr_w[0].bitcast(FP)[:, j, :], op0=ALU.mult, op1=ALU.subtract)
            ins.then_inc(lr_split, 1)
            for p in range(2):
                dve.wait_ge(sq_done, 2 * p + 2)
                root_steps(c, RSQ * p, DM, slice(2 * p, 2 * p + 2))
                normalised(c, p)
            for p in range(2):
                transposed_lo(c, p, 0)
            lo(c, 0, FIRST_QK[0])
            lo(c, 1, FIRST_QK[1])
            dve.wait_ge(at_full, KC + 1)
            dve.wait_ge(ones_set, 1)
            nc.vector.tensor_copy(lrT[0:RANK, :], AT[KC % 4][0:RANK, :]).then_inc(at_fd, 1)
            for b in range(NB):
                dve.wait_ge(at_full, KC + 2 + b)
                t = AT[(KC + 1 + b) % 4]
                nc.vector.tensor_scalar(gate[:, b, :].bitcast(I32), t[:, :].bitcast(I32), 0x7FFFFFFF, None,
                                        ALU.bitwise_and).then_inc(u_abs, 1)
            for b in range(NB):
                dve.wait_ge(u_ln, b + 1)
                nc.vector.scalar_tensor_tensor(out=lgate[:, b, :], in0=AT[(KC + 1 + b) % 4][:, :], scalar=0.0,
                                               in1=lgate[:, b, :], op0=ALU.min, op1=ALU.subtract).then_inc(at_fd, 1)

            def add_out(c, tile, count, first=0, end=8):
                for t in range(first, end):
                    dve.wait_ge(pj_full, c("pj_full", count + t + 1))
                    o = x1[:, t // 2, (t % 2) * 512:(t % 2) * 512 + 512]
                    nc.vector.tensor_tensor(o, PJ[(tile + t) % 4][:, :], o, ALU.add).then_inc(pj_fd, 1)

            def head(h, c, last=False, nxt=None):
                units = head_units(h, last) + [nxt(h)]

                def value_lo(u):
                    for i in range(2):
                        t = 2 * u + i
                        dve.wait_ge(vh, c("vh", t + 1))
                        w = (slice(None), slice(2 * i, 2 * i + 2), slice(u * UW, (u + 1) * UW))
                        nc.vector.tensor_tensor(vr[1][w], PJ[t % 4][:, :].rearrange("p (s c) -> p s c", s=2),
                                                vr[0].bitcast(FP)[w], ALU.subtract).then_inc(pj_fd, 1)

                def gates(i):
                    dve.wait_ge(th, c("th", i + 1))
                    nc.vector.scalar_tensor_tensor(
                        out=gate[:, 2 * i:2 * i + 2, 0:UW], in0=scr[:, i, :].rearrange("p (s c) -> p s c", s=2),
                        scalar=1.0, in1=PJ[i % 4][:, :].rearrange("p (s c) -> p s c", s=2),
                        op0=ALU.add, op1=ALU.mult).then_inc(pj_fd, 1)

                def gated(i):
                    dve.wait_ge(th, c("th", i + 3))
                    nc.vector.scalar_tensor_tensor(out=scr[:, i, :], in0=scr[:, i, :], scalar=1.0, in1=PJ[2 + i][:, :],
                                                   op0=ALU.add, op1=ALU.mult).then_inc(pj_fd, 1)
                    dve.wait_ge(pj_fd, c("pj_fd", 7 + i))
                    o = gate[:, 2 * i:2 * i + 2, UW:2 * UW]
                    nc.vector.tensor_tensor(o, o, scr[:, i, :].rearrange("p (s c) -> p s c", s=2),
                                            ALU.mult).then_inc(g2, 1)

                def oT_lo(i):
                    dve.wait_ge(oth, c("oth", i + 1))
                    nc.vector.tensor_tensor(oT[1][:, i, :], AT[c.parity("at_slots", NL + 7 + i, 4)][:, :],
                                            oT[0].bitcast(FP)[:, i, :], ALU.subtract).then_inc(at_fd, 1)

                def decay(i):
                    dve.wait_ge(lve, c("lve", i + 1 + (i == NL - 1)))
                    w = max(i - 1, 0)
                    dve.wait_ge(at_full, c("at_full", w))
                    for u in range(2):
                        d, s, e = (t.rearrange("p (n u l) -> p n u l", u=2, l=LEVELS[i])[:, :, u, :]
                                   for t in (qkd[:, i % 2, :], qk[:, 1 - u, :], ee[:, i % 2, :]))
                        ins = nc.vector.tensor_tensor(d, s, e, ALU.mult)
                    ins.then_inc(lvq, 1)

                def keep(i):
                    dve.wait_ge(at_full, c("at_full", i + 1))
                    if i == 0:
                        dve.wait_ge(dv, c("dv", 1))
                    else:
                        dve.wait_ge(at_fd, c("at_fd", i))
                    nc.vector.memset(tick, 0.0)
                    m = cst[:, C_MASK + i * P:C_MASK + (i + 1) * P].bitcast(I32)
                    new = AT[c.parity("at_slots", i, 4)]
                    if i == NL:
                        nc.vector.copy_predicated(atd[:, :, :], m.unsqueeze(1).to_broadcast([P, NB, P]),
                                                  new[:, :].rearrange("p (b t) -> p b t", b=NB)).then_inc(at_fd, 1)
                        return
                    L = LEVELS[i]
                    n = P // (2 * L)
                    for b in range(NB):
                        ins = nc.vector.copy_predicated(
                            atd[:, b, :].rearrange("p (n u l) -> p n u l", u=2, l=L)[:, :, 1, :],
                            m.rearrange("p (n u l) -> p n u l", u=2, l=L)[:, :, 1, :],
                            new[:, b * 64:b * 64 + 64].rearrange("p (n l) -> p n l", l=L))
                    ins.then_inc(at_fd, 1)

                nc.vector.memset(atd[:, :, :], 0.0).then_inc(dv, 1)
                dve.wait_ge(pj_fa, c("pj_fa", 0))
                decay(0)
                decay(1)
                lo(c, 1, units[1])
                keep(0)
                decay(2)
                value_lo(0)
                keep(1)
                decay(3)
                keep(2)
                lo(c, 2, units[2])
                decay(4)
                keep(3)
                decay(5)
                value_lo(1)
                decay(6)
                q4, k4 = (qk[:, i, :].rearrange("p (b t) -> p b t", b=NB) for i in range(2))
                v = nc.vector
                v.tensor_tensor(qd[:, 0:2, :], q4[:, 1:3, :], e1[:, 0:2, :], ALU.mult)
                v.tensor_tensor(qd[:, 3, :], q4[:, 3, :], e1[:, 2, :], ALU.mult)
                link(c, 1, v.tensor_tensor(kd[:, 0:3, :], k4[:, 0:3, :], e2[:, :, :], ALU.mult))
                v.tensor_scalar(qd[:, 2, :], qd[:, 3, :], etot[:, 2:3], None, ALU.mult)
                v.tensor_scalar(kd[:, 3, :], kd[:, 0, :], etot[:, 1:2], None, ALU.mult).then_inc(qd_done, 1)
                keep(4)
                keep(5)
                lo(c, 3, units[3])
                keep(6)
                keep(7)
                dve.wait_ge(at_fd, c("at_fd", NL + 1))
                dve.wait_ge(at_hi, c("at_hi", 1))
                nc.vector.tensor_tensor(at[1][:, 0:4, :], atd[:, :, :], at[0][:, 0:4, :].bitcast(FP),
                                        ALU.subtract).then_inc(ats, 1)
                dve.wait_ge(at_hi, c("at_hi", 2))
                for i in range(2):
                    w = slice(4 + 3 * i, 7 + 3 * i)
                    nc.vector.tensor_tensor(at[1][:, w, :].rearrange("p a b -> p (a b)"),
                                            AT[c.parity("at_slots", NL + 1 + i, 4)][:, 0:384],
                                            at[0][:, w, :].bitcast(FP).rearrange("p a b -> p (a b)"),
                                            ALU.subtract).then_inc(at_fd, 1)
                gates(0)
                gates(1)
                lo(c, 4, units[4])
                dve.wait_ge(head_sq, c("sq", 4))
                dve.wait_ge(pj_fd, c("pj_fd", 6))
                root_steps(c, 2, DV)
                link(c, 2 + RSQ, v.tensor_scalar(rstd, rstd, 0.5, None, ALU.mult))
                o_tiles = [AT[c.parity("at_slots", NL + 3 + i, 4)] for i in range(NB)]
                for i in range(NB):
                    nc.vector.scalar_tensor_tensor(out=gate[:, i, 0:UW], in0=o_tiles[i][:, 0:UW],
                                                   scalar=rstd[:, i:i + 1], in1=gate[:, i, 0:UW],
                                                   op0=ALU.mult, op1=ALU.mult).then_inc(og, 1)
                for i in range(NB):
                    nc.vector.tensor_scalar(gate[:, i, UW:2 * UW], o_tiles[i][:, UW:2 * UW], rstd[:, i:i + 1], None,
                                            ALU.mult).then_inc(at_fd, 1)
                dve.wait_ge(at_fd, c("at_fd", NL + 7))
                gated(0)
                if last:
                    oT_lo(0)
                    oT_lo(1)
                    gated(1)
                    lo(c, 5, units[5])
                    add_out(c, 8, 8, 0, 4)
                    oT_lo(2)
                    oT_lo(3)
                    add_out(c, 8, 8, 4, 8)
                else:
                    gated(1)
                    lo(c, 5, units[5])
                    lo(c, 6, units[6])
                    for i in range(4):
                        oT_lo(i)
                    lo(c, 7, units[7])
                    add_out(c, 12, 10)
                if last:
                    add_out(c, 16, 16, 0, 1)
                    lo(c, 6, units[6], (0,))
                    add_out(c, 16, 16, 1, 4)
                else:
                    add_out(c, 20, 18, 0, 2)
                    lo(c, 8, units[8], (0,))
                    add_out(c, 20, 18, 2, 4)
                    lo(c, 8, units[8], (1,))
                    add_out(c, 20, 18, 4, 8)

            lo(c, 2, v_a(0, 0))
            dve.wait_ge(m_in, 16)
            turns(dve, 0, GH - 1, B_HEAD, HEAD, lambda h, c: head(h, c, nxt=lambda h: v_a(h + 1, 0)))
            head(GH - 1, Span(B_LAST, LAST), True, nxt=lambda h: FIRST_UNITS[0])

            c = Span(B_MID, MID)
            add_last(c, -8, 2 * NB)
            normalised(c, 0)
            add_out(c, 0, -8, 6, 8)
            lo(Span(B_LAST, LAST), 6, FIRST_UNITS[0], (1,))
            transposed_lo(c, 0, KC)
            dve.wait_ge(sq_done, 2 * NB)
            root_steps(c, RSQ, DM, slice(2, 4))
            normalised(c, 1)
            transposed_lo(c, 1, KC)

            def swap(c, k, dst, src):
                for a in range(4):
                    for b in range(4):
                        ins = nc.vector.tensor_copy(dst[32 * a:32 * a + 32, :, b], src[32 * b:32 * b + 32, :, a])
                link(c, k, ins)

            def attended(c, dst=oT2):
                for j in range(2):
                    dve.wait_ge(at_fa, c("at_fa", 5 + j))
                    dve.wait_ge(at_full, c("at_full", 10 + 2 * j))
                    o = o_sum[:, j, :]
                    by_class = o.rearrange("p (j r) -> p r j", r=4)
                    nc.vector.tensor_tensor(by_class, AT[c.parity("at_slots", 9 + 2 * j, 4)][:, :].rearrange(
                        "p (r j) -> p r j", r=4), by_class, ALU.add).then_inc(at_fd, 1)
                    dve.wait_ge(at_fd, c("at_fd", 5 + j))
                    nc.vector.tensor_tensor(o, o, gate2[:, j, :], ALU.mult).then_inc(og2, 1)
                for j in range(2):
                    dve.wait_ge(ob, c("ob", j + 1))
                    nc.vector.tensor_tensor(dst[1][:, j, :], o_sum[:, j, :], dst[0][:, j, :].bitcast(FP),
                                            ALU.subtract).then_inc(ot2, 1)

            def batch(n, c, first=False, out=True, nxt=None):
                units = (FIRST_UNITS if first else batch_units(n, out)) + [nxt]
                d = 1 if first else 0
                a0 = 0 if first else 12

                def bias0():
                    for j in range(2):
                        sl = slopes(n, j)
                        t0, t1 = (AT[c.parity("at_slots", a0 + 2 * j + i, 4)] for i in range(2))
                        d = cst[:, C_DIST:C_DIST + 256]
                        dve.wait_ge(at_full, c("at_full", a0 + 2 * j + 1))
                        nc.vector.scalar_tensor_tensor(out=s0[:, j, 0:128], in0=d[:, 128:256], scalar=sl,
                                                       in1=t0[:, 0:128], op0=ALU.mult, op1=ALU.add)
                        nc.vector.scalar_tensor_tensor(out=s0[:, j, 128:384], in0=d, scalar=sl,
                                                       in1=t0[:, 128:384], op0=ALU.mult, op1=ALU.add).then_inc(at_fd, 1)
                        dve.wait_ge(at_full, c("at_full", a0 + 2 * j + 2))
                        nc.vector.scalar_tensor_tensor(
                            out=s0[:, j, 384:896].rearrange("p (a k) -> p a k", a=2),
                            in0=d.unsqueeze(1).to_broadcast([P, 2, 256]), scalar=sl,
                            in1=t1[:, :].rearrange("p (a k) -> p a k", a=2), op0=ALU.mult, op1=ALU.add).then_inc(at_fd, 1)

                def bias12(g):
                    for j in range(2):
                        t = a0 + 4 + 2 * (g - 1) + j
                        d = cst[:, C_DIST + 128 + 128 * g:C_DIST + 256 + 128 * g]
                        dve.wait_ge(at_full, c("at_full", t + 1))
                        nc.vector.scalar_tensor_tensor(
                            out=s12[j][:, :, 128 * (g - 1):128 * g], in0=d.unsqueeze(1).to_broadcast([P, 4, 128]),
                            scalar=slopes(n, j), in1=AT[c.parity("at_slots", t, 4)][:, :].rearrange("p (r k) -> p r k", r=4),
                            op0=ALU.mult, op1=ALU.add).then_inc(at_fd, 1)

                if first:
                    lo(c, 1, units[1])
                lo(c, 1 + d, units[1 + d])
                if not first:
                    probs_out(c)
                lo(c, 2 + d, units[2 + d])
                if not first:
                    attended(c)
                lo(c, 3 + d, units[3 + d])
                bias0()
                k, t = 3 + d, 6 + 2 * d
                if out:
                    lo(c, 4, units[4])
                    add_out(c, 6, 6)
                    k, t = 4, 14
                lo(c, k + 1, units[k + 1])
                lo(c, k + 2, units[k + 2])
                bias12(1)
                lo(c, k + 3, units[k + 3])
                if first:
                    k, t = k - 1, t - 2
                else:
                    lo(c, k + 4, units[k + 4])
                bias12(2)
                lo(c, k + 5, units[k + 5])
                dve.wait_ge(at_fd, c("at_fd", 8 if first else 14))
                v = nc.vector
                for j in range(2):
                    v.tensor_reduce(mx[:, 0, j, 0:1], s0[:, j, 0:128], AX.X, ALU.max)
                    v.tensor_reduce(mx[:, 0, j, 1:4], s0[:, j, 128:896].rearrange("p (b k) -> p b k", b=3), AX.X, ALU.max)
                    ins = v.tensor_reduce(mx[:, 1, j, :], s12[j][:, :, :], AX.X, ALU.max)
                link(c, 0, ins)
                swap(c, 1, xch[:, 0], mx[:, 1])
                link(c, 2, v.tensor_tensor(mx[:, 0], mx[:, 0], xch[:, 0], ALU.max))
                swap(c, 3, mx[:, 1], mx[:, 0])
                v.tensor_scalar(nbias[:, :, :, :], mx[:, :, :, :], -QK_SCALE, None, ALU.mult).then_inc(nb_done, 1)
                lo(c, k + 6, units[k + 6])

                def gate_of(j):
                    dve.wait_ge(zt, c("zt", j + 1))
                    v.scalar_tensor_tensor(out=gate2[:, j, :], in0=scr[:, j, :], scalar=1.0, in1=PJ[(t + 12 + j) % 4][:, :],
                                           op0=ALU.add, op1=ALU.mult).then_inc(pj_fd, 1)

                dve.wait_ge(ex_done, c("ex", 1))
                swap(c, 4, xch[:, 0], lsum[:, 1])
                link(c, 5, v.tensor_tensor(lsum[:, 0], lsum[:, 0], xch[:, 0], ALU.add))
                swap(c, 6, lsum[:, 1], lsum[:, 0])
                link(c, 7, v.tensor_scalar(lsum[:, :, :, :], lsum[:, :, :, :], 2.0, None, ALU.mult))
                link(c, 8, v.reciprocal(rinv[:, :, :, :], lsum[:, :, :, :]))
                lo(c, k + 7, units[k + 7])
                gate_of(0)
                lo(c, k + 8, units[k + 8])
                for j in range(2):
                    for b in range(NB):
                        w = slice(max(256 * b - 128, 0), 256 * b + 128)
                        v.tensor_scalar(s0[:, j, w], s0[:, j, w], rinv[:, 0, j, b:b + 1], None, ALU.mult)
                        ins = v.tensor_scalar(s12[j][:, b, :], s12[j][:, b, :], rinv[:, 1, j, b:b + 1], None, ALU.mult)
                ins.then_inc(nrm_done, 1)
                gate_of(1)

            def slopes(n, j):
                return cst[:, bass.ds(n * 2 + (C_SLOPE + j), 1)]

            def probs_out(c):
                for t in range(1, 8, 2):
                    w = 512 if t < 7 else 256
                    dve.wait_ge(at_full, c("at_full", t + 1))
                    nc.vector.tensor_copy(pT[:, 4 * t:4 * t + w // P, :].rearrange("p a b -> p (a b)"),
                                          AT[c.parity("at_slots", t, 4)][:, 0:w]).then_inc(at_fd, 1)

            batch(0, Span(B_FIRST, FIRST), True, False, batch_units(1, True)[0])
            turns(dve, 1, BATCHES - 1, B_BATCH, BATCH,
                  lambda n, c: batch(n, c, nxt=batch_units(n + 1, True)[0]))
            batch(BATCHES - 1, Span(B_FINAL, FINAL), out=False, nxt=TAIL_OUT[0])
            c = Span(B_TAIL, TAIL)
            probs_out(c)
            lo(c, 1, TAIL_OUT[1])
            add_out(c, 0, 0, 0, 3)
            attended(c, oT2_last)
            add_out(c, 0, 0, 3, 8)
            add_out(c, 0, 8, 0, 4)
            add_last(c, 8, 3 * NB)
            add_out(c, 0, 8, 6, 8)
            for b in (0, 2):
                if b:
                    dve.wait_ge(sq_done, 3 * NB)
                    root_steps(c, RSQ, DM, slice(2, 4))
                dve.wait_ge(xg_done, b + 1)
                nc.vector.tensor_scalar(xg[:, b, :], xg[:, b, :], rstd[:, b:b + 1], None, ALU.mult).then_inc(y_done[b], 1)

        @block.tensor
        def _(pe):
            def ring(c, plan, name, t, banks, fa, fd, fan, fdn, tail):
                p = t - 4
                while p >= 0 and plan[p] is None:
                    p -= 4
                for who, s, sn in (("A", fa, fan), ("D", fd, fdn)):
                    if p < 0 and tail is not None:
                        if tail[p] == who:
                            pe.wait_ge(s, c(sn, -tail[p:].count(who) + 1))
                    elif p >= 0:
                        if plan[p] == who:
                            pe.wait_ge(s, c(sn, plan[:p + 1].count(who)))
                    else:
                        w = c(sn, 0)
                        if not isinstance(w, int) or w:
                            pe.wait_ge(s, w)
                return banks[c.parity(name, t, 4)]

            def pj(c, plan, t):
                tail = BY_BATCH if c.before.get("nb", 0) else ALL_D
                return ring(c, plan, "pj_slots", t, PJ, pj_fa, pj_fd, "pj_fa", "pj_fd", tail)

            def att(c, plan, t):
                return ring(c, plan, "at_slots", t, AT, at_fa, at_fd, "at_fa", "at_fd", None)

            def product(out_ap, stat_, mov, start, stop):
                for i, (a, b) in enumerate(((0, 0), (0, 1), (1, 0))):
                    ins = nc.tensor.matmul(out_ap, stat_[a], mov[b], start=start and i == 0, stop=stop and i == 2)
                return ins

            def weights(c, k, unit):
                slot = c.parity("unit", k, 2)
                return [unit_view(t[slot], unit) for t in (whi, wlo)]

            def split(c, k, m):
                pe.wait_ge(lo_done, c("halves", 2 * k + m + 1))

            def features_out(c, plan, k, unit, tile, beside=None):
                w = weights(c, k, unit)
                for m in range(unit[2] // P):
                    o = pj(c, plan, tile + m)
                    for kk in range(KC):
                        if m == 0 and kk % (KC // 2) == 0:
                            split(c, k, kk // (KC // 2))
                        ins = product(o[:, :], [x_[:, kk, m * P:(m + 1) * P] for x_ in w],
                                      [t[:, kk, :] for t in hT], kk == 0, kk == KC - 1)
                        if beside:
                            beside(kk)
                    ins.then_inc(pj_full, 1)

            def tokens_out(c, plan, k, unit, tile, pick, midway=None, parts=None):
                w = weights(c, k, unit)
                for s in range(NB):
                    if s % 2 == 0:
                        o = pj(c, plan, tile + s // 2)
                    for kk in range(KC):
                        if s == 0 and kk % (KC // 2) == 0:
                            split(c, k, kk // (KC // 2))
                        if parts is not None and s % 2 == 0 and kk % 2 == 0:
                            pe.wait_ge(at_fd, parts + 2 * s + kk // 2 + 1)
                        ins = product(o[:, (s % 2) * UW:(s % 2 + 1) * UW], [pick(t, kk, s) for t in hT],
                                      [x_[:, kk, :] for x_ in w], kk == 0, kk == KC - 1)
                    if s % 2 == 1:
                        ins.then_inc(pj_full, 1)
                    if s == 1 and midway:
                        midway()

            def out_proj(c, plan, k, unit, tile, o_parts, c0, midway=None, tiles=range(8)):
                w = weights(c, k, unit)
                for t in tiles:
                    s, nh = t // 2, t % 2
                    o = pj(c, plan, tile + t)
                    for cc in range(2):
                        if t == 0:
                            split(c, k, cc)
                        ins = product(o[:, :], [x_[:, c0 + cc, s * P:(s + 1) * P] for x_ in o_parts],
                                      [x_[:, cc, nh * 512:(nh + 1) * 512] for x_ in w], cc == 0, cc == 1)
                    ins.then_inc(pj_full, 1)
                    if t == 3 and midway:
                        midway()

            def block_of(t, kk, s):
                return t[:, kk, s * P:(s + 1) * P]

            def class_of(t, kk, s):
                return t[:, kk, s:SEQ:4]

            def rows_transposed(c, plan, turn, p):
                pe.wait_ge(xn_a, 2 * turn + p + 1)
                pe.wait_ge(xn_d, 2 * turn + p + 1)
                for k in range(4):
                    o = att(c, plan, 4 * p + k)
                    for m in range(4):
                        f, b = 2 * k + m // 2, 2 * p + m % 2
                        ins = nc.tensor.transpose(o[:, m * P:(m + 1) * P], big[:, b, f * P:(f + 1) * P], ident)
                    ins.then_inc(at_full, 1)

            c = Span(B_PRO, PRO)
            pe.wait_ge(c_in, 16)
            rows_transposed(c, AT_PRO, 0, 0)
            rows_transposed(c, AT_PRO, 0, 1)
            pe.wait_ge(lr_split, 1)
            o = att(c, AT_PRO, KC)
            for kk in range(KC):
                pe.wait_ge(at_fd, 5 + kk // 2)
                ins = product(o[0:RANK, :], [t[:, kk, :] for t in lr_w], [t[:, kk, :] for t in hT], kk == 0, kk == KC - 1)
            ins.then_inc(at_full, 1)

            def gate_logits(kk):
                b = kk - 3
                if b == 0:
                    pe.wait_ge(at_fd, KC + 1)
                    pe.wait_ge(wup_in, 16)
                if 0 <= b < NB:
                    o = att(c, AT_PRO, KC + 1 + b)
                    nc.tensor.matmul(o[:, :], lrT[0:RANK + 1, b * P:(b + 1) * P], wup[0:RANK + 1, :],
                                     start=True, stop=True).then_inc(at_full, 1)

            features_out(c, PJ_PRO, 0, FIRST_QK[0], 0, beside=gate_logits)
            features_out(c, PJ_PRO, 1, FIRST_QK[1], 2)
            pe.wait_ge(at_fd, KC + 5)
            for h in range(GH):
                o = att(c, AT_PRO, KC + 5 + h)
                for b in range(NB):
                    ins = nc.tensor.matmul(o[:, b * P:(b + 1) * P], lgate[:, b, h * P:(h + 1) * P], tri,
                                           start=True, stop=True)
                ins.then_inc(at_full, 1)

            def head(h, c, last=False):
                units = head_units(h, last)
                plan = PJ_LAST if last else PJ_HEAD

                def level(i):
                    o = att(c, AT_HEAD, i)
                    if i < NL:
                        pe.wait_ge(lvq, c("lvq", i + 1))
                    for b in range(NB):
                        w = slice(b * P, (b + 1) * P)
                        if i < NL:
                            d = qkd[:, i % 2, w]
                            q = d.rearrange("p (n u l) -> p n u l", u=2, l=LEVELS[i])[:, :, 1, :]
                            ins = nc.tensor.matmul(o[:, b * 64:b * 64 + 64].rearrange("p (n l) -> p n l", l=LEVELS[i]),
                                                   d, q, start=True, stop=True)
                        else:
                            ins = nc.tensor.matmul(o[:, w], qk[:, 1, w], qk[:, 0, w], start=True, stop=True)
                    ins.then_inc(at_full, 1)

                def last_levels():
                    level(NL - 1)
                    level(NL)
                    pe.wait_ge(qd_done, c("qd", 1))
                    o = att(c, AT_HEAD, NL + 1)
                    nc.tensor.matmul(o[:, 0:128], kd[:, 0, :], qd[:, 0, :], start=True, stop=True)
                    nc.tensor.matmul(o[:, 128:384], kd[:, 3, :], qd[:, 1:3, :].rearrange("p a b -> p (a b)"),
                                     start=True, stop=True).then_inc(at_full, 1)
                    o = att(c, AT_HEAD, NL + 2)
                    nc.tensor.matmul(o[:, 0:256], kd[:, 1, :], qd[:, 1:3, :].rearrange("p a b -> p (a b)"),
                                     start=True, stop=True)
                    nc.tensor.matmul(o[:, 256:384], kd[:, 2, :], qd[:, 3, :], start=True, stop=True).then_inc(at_full, 1)

                def turn(i):
                    if i < 2:
                        pe.wait_ge(og, c("og", 4))
                    else:
                        pe.wait_ge(g2, c("g2", 2))
                    o = att(c, AT_HEAD, NL + 7 + i)
                    for b in range(NB):
                        ins = nc.tensor.transpose(o[:, b * P:(b + 1) * P], gate[:, b, i * P:(i + 1) * P], ident)
                    ins.then_inc(at_full, 1)

                pe.wait_ge(pj_fa, c("pj_fa", 0))
                tokens_out(c, plan, 0, units[0], 0, block_of, lambda: level(0))
                level(1)
                level(2)
                tokens_out(c, plan, 1, units[1], 2, block_of, lambda: level(3))
                level(4)
                level(5)
                tokens_out(c, plan, 2, units[2], 4, block_of, last_levels)
                pe.wait_ge(ats, c("ats", 1))
                pe.wait_ge(at_fd, c("at_fd", NL + 3))
                pe.wait_ge(pj_fd, c("pj_fd", 4))
                between = {(0, 1): 4, (0, 2): 5, (0, 3): 6, (1, 2): 7, (1, 3): 8, (2, 3): 9}
                for i in range(NB):
                    o = att(c, AT_HEAD, NL + 3 + i)
                    for j in range(i + 1):
                        k = i if j == i else between[j, i]
                        ins = product(o[:, :], [t[:, k, :] for t in at], [t[:, j, :] for t in vr], j == 0, j == i)
                    ins.then_inc(at_full, 1)
                if last:
                    tokens_out(c, plan, 3, units[3], 6, block_of, lambda: (turn(0), turn(1)))
                    pe.wait_ge(at_fd, c("at_fd", NL + 9))
                    out_proj(c, plan, 4, units[4], 8, oT, 0, lambda: (turn(2), turn(3)))
                    pe.wait_ge(at_fd, c("at_fd", NL + 11))
                    out_proj(c, plan, 5, units[5], 16, oT, 2)
                    return
                tokens_out(c, plan, 3, units[3], 6, block_of)
                features_out(c, plan, 4, units[4], 8)
                for i in range(4):
                    turn(i)
                features_out(c, plan, 5, units[5], 10)
                pe.wait_ge(at_fd, c("at_fd", NL + 11))
                out_proj(c, plan, 6, units[6], 12, oT, 0)
                out_proj(c, plan, 7, units[7], 20, oT, 2)

            turns(pe, 0, GH - 1, B_HEAD, HEAD, head)
            head(GH - 1, Span(B_LAST, LAST), True)
            rows_transposed(Span(B_MID, MID), AT_MID, 1, 0)

            def turned(c, plan):
                blocks = []
                for j in range(2):
                    blocks += [s0[:, j, b * P:(b + 1) * P] for b in range(7)]
                    blocks += [s12[j][:, r, g * P:(g + 1) * P] for r in range(4) for g in range(2)]
                pe.wait_ge(nrm_done, c("nrm", 0))
                for t in range(8):
                    o = att(c, plan, t)
                    for i, p in enumerate(blocks[4 * t:4 * t + 4]):
                        ins = nc.tensor.transpose(o[:, i * P:(i + 1) * P], p, ident)
                    ins.then_inc(at_full, 1)

            def attend(c, plan):
                pe.wait_ge(at_fa, c("at_fa", 4))
                pe.wait_ge(at_fd, c("at_fd", 4))
                for j in range(2):
                    w = slice(j * P, (j + 1) * P)
                    o = att(c, plan, 8 + 2 * j)
                    for b in range(NB):
                        d = o[:, b * P:(b + 1) * P]
                        if b:
                            nc.tensor.matmul(d, vv[0][:, b - 1, w], pT[:, 15 * j + 2 * b - 1, :], start=True, stop=False)
                        ins = nc.tensor.matmul(d, vv[0][:, b, w], pT[:, 15 * j + 2 * b, :], start=b == 0, stop=True)
                    ins.then_inc(at_full, 1)
                    o = att(c, plan, 9 + 2 * j)
                    for r in range(4):
                        d = o[:, r * P:(r + 1) * P]
                        for g in range(2):
                            ins = nc.tensor.matmul(d, vv[1 + g][:, r, w], pT[:, 15 * j + 7 + 2 * r + g, :],
                                                   start=g == 0, stop=g == 1)
                    ins.then_inc(at_full, 1)

            def batch(n, c, first=False, out=True):
                units = FIRST_UNITS if first else batch_units(n, out)
                d = 1 if first else 0
                pj_plan, at_plan = PJ_BATCH if out else PJ_FIRST, AT_FIRST if first else AT_BATCH
                a0 = 0 if first else 12

                def scores(g):
                    q, k = qT[g % 2], kT[g % 2]
                    pe.wait_ge(pj_fa, c("pj_fa", 4 * g + 4 + 2 * d))
                    for j in range(2):
                        if g == 0:
                            for half in range(2):
                                o = att(c, at_plan, a0 + 2 * j + half)
                                for b in (2 * half, 2 * half + 1):
                                    kw = slice(max(b - 1, 0) * P, (b + 1) * P)
                                    at0 = (0, 128, 0, 256)[b]
                                    ins = nc.tensor.matmul(o[:, at0:at0 + kw.stop - kw.start], q[:, j, b * P:(b + 1) * P],
                                                           k[:, j, kw], start=True, stop=True)
                                ins.then_inc(at_full, 1)
                        else:
                            o = att(c, at_plan, a0 + 2 + 2 * g + j)
                            for r in range(4):
                                w = slice(r * P, (r + 1) * P)
                                ins = nc.tensor.matmul(o[:, w], q[:, j, w], k[:, j, w], start=True, stop=True)
                            ins.then_inc(at_full, 1)

                if first:
                    tokens_out(c, pj_plan, 0, units[0], 0, block_of,
                               lambda: rows_transposed(Span(B_MID, MID), AT_MID, 1, 1), B_MID["at_fd"])
                features_out(c, pj_plan, d, units[d], 2 * d)
                if not first:
                    turned(c, at_plan)
                features_out(c, pj_plan, 1 + d, units[1 + d], 2 + 2 * d)
                if not first:
                    attend(c, at_plan)
                features_out(c, pj_plan, 2 + d, units[2 + d], 4 + 2 * d)
                scores(0)
                k, t = 3 + d, 6 + 2 * d
                if out:
                    pe.wait_ge(ot2, c("ot2", 2))
                    out_proj(c, pj_plan, 3, units[3], 6, oT2, 0)
                    k, t = 4, 14
                features_out(c, pj_plan, k, units[k], t)
                features_out(c, pj_plan, k + 1, units[k + 1], t + 2)
                scores(1)
                features_out(c, pj_plan, k + 2, units[k + 2], t + 4)
                if first:
                    k, t = k - 1, t - 2
                else:
                    tokens_out(c, pj_plan, k + 3, units[k + 3], t + 6, block_of)
                scores(2)
                tokens_out(c, pj_plan, k + 4, units[k + 4], t + 8, class_of)
                tokens_out(c, pj_plan, k + 5, units[k + 5], t + 10, class_of)
                features_out(c, pj_plan, k + 6, units[k + 6], t + 12)
                features_out(c, pj_plan, k + 7, units[k + 7], t + 13)

            batch(0, Span(B_FIRST, FIRST), True, False)
            turns(pe, 1, BATCHES - 1, B_BATCH, BATCH, batch)
            batch(BATCHES - 1, Span(B_FINAL, FINAL), out=False)
            c = Span(B_TAIL, TAIL)
            plan = ["D"] * 16

            def earlier_out(tiles):
                out_proj(c, plan, 0, TAIL_OUT[0], 0, oT2, 0, tiles=tiles)

            earlier_out(range(0, 3))
            turned(c, AT_BATCH)
            earlier_out(range(3, 4))
            attend(c, AT_BATCH)
            earlier_out(range(4, 8))
            pe.wait_ge(ot2, c("ot2", 2))
            out_proj(c, plan, 1, TAIL_OUT[1], 8, oT2_last, 0)


def constants():
    import numpy as np
    t = np.zeros((P, C_END), np.float32)
    i = np.arange(P)
    t[:, C_ID:C_ID + P] = np.eye(P)
    t[:, C_TRI:C_TRI + P] = np.where(i[:, None] <= i[None, :], 1 / 16.0, 0.0)
    tok = 4 * (i % 32) + i // 32
    own = tok[:, None] - i[None, :]
    cls = i[:, None] - i[None, :]
    far = 1e30
    step = 2.0 ** (-8.0 / GROUPS)
    t[:, C_DIST:C_DIST + 128] = np.where(own <= 0, own + 128.0, far)
    t[:, C_DIST + 128:C_DIST + 256] = np.where(own >= 0, own * 1.0, far)
    t[:, C_DIST + 256:C_DIST + 384] = np.where(cls >= 0, cls * 4.0 * step, far)
    t[:, C_DIST + 384:C_DIST + 512] = np.where((cls >= 0) & (cls % 4 == 0), cls * 4.0 * step ** 2, far)
    s, u = i[:, None], i[None, :]
    for k, L in enumerate(LEVELS):
        pair = (s // (2 * L) == u // (2 * L)) & (s % (2 * L) < L) & (u % (2 * L) >= L)
        t[:, C_MASK + k * P:C_MASK + (k + 1) * P] = pair
    t[:, C_MASK + NL * P:C_MASK + (NL + 1) * P] = np.eye(P)
    h = np.arange(HEADS)
    t[:, C_SLOPE:C_SLOPE + HEADS] = -(2.0 ** (-8.0 * (h + 1) / (GROUPS * HEADS))) / QK_SCALE
    return t


def kernel(x, a_norm, a_w_in, a_w_gate_up, a_b_gate, a_g_out, a_w_out, kv_norm, w_kv, b_norm, b_w_in, b_w_out,
           final_norm):
    import numpy as np
    import concourse.bacc as bacc
    from concourse.bass_utils import run_bass_kernel_spmd

    a = {n: np.ascontiguousarray(v) for n, v in dict(
        x=x[0], a_w_in=a_w_in[0], w_gate_up=np.concatenate([a_w_gate_up[0], a_b_gate[0:1]], 0), a_w_out=a_w_out[0],
        w_kv=w_kv, b_w_in=b_w_in[0], b_w_out=b_w_out[0],
        gains=np.concatenate([np.asarray(g).reshape(-1, P).T for g in (a_norm[0], kv_norm, b_norm[0], a_g_out[0])], 1),
        final_norm=final_norm, consts=constants()).items()}
    nc = bacc.Bacc("TRN2", target_bir_lowering=False, num_devices=1, dynamic_dma_scratch_size=1024)
    aps = [nc.dram_tensor(f"in_{n}", v.shape, mybir.dt.from_np(v.dtype), kind="ExternalInput").ap() for n, v in a.items()]
    o = nc.dram_tensor("out_y", (SEQ, DM), FP, kind="ExternalOutput").ap()
    trunk(nc, *aps, o)
    r = run_bass_kernel_spmd(nc, [{f"in_{n}": v for n, v in a.items()}], core_ids=[0])
    return r.results[0]["out_y"].reshape(1, SEQ, DM)
```
